# Optimizing a Trainium2 kernel written in Bass

```python
import jax
import jax.numpy as jnp
from jax import lax
import numpy as np
import math

D_MODEL = 2048
BATCH = 1
SEQ = 256
DEPTH = 1

EPS = 1e-6
HEAD_DIM = 128

GLA_HEADS = 4
GLA_DK = 64
GLA_DV = 128
GLA_GATE_RANK = 16
GLA_TAU = 16.0
GLA_CHUNK = 64

DIL_HEADS = 12
DIL_PATTERNS = ((128, 1), (512, 4), (2048, 16))
ROPE_THETA = 500000.0
ROPE_DIM = HEAD_DIM // 4
MASK_VALUE = -1e30

PEER_HEADS = 8
PEER_NKEYS = 128
PEER_NEXPERTS = PEER_NKEYS * PEER_NKEYS
PEER_QDIM = 256
PEER_TOPK = 16
PEER_TOKEN_BLOCK = 128

GLA_QK_W = GLA_HEADS * GLA_DK
GLA_V_W = GLA_HEADS * GLA_DV
DIL_W = DIL_HEADS * HEAD_DIM
MIX_W = GLA_V_W + DIL_W
IN_SPLITS = (GLA_QK_W, GLA_QK_W, GLA_V_W, GLA_GATE_RANK, GLA_GATE_RANK, GLA_V_W, DIL_W, DIL_W, DIL_W)
IN_W = sum(IN_SPLITS)


def rms_norm(x, g):
    xf = x.astype(jnp.float32)
    y = xf * lax.rsqrt(jnp.mean(xf * xf, axis=-1, keepdims=True) + EPS)
    return (y * g.astype(jnp.float32)).astype(x.dtype)

def partial_rope(t, positions):
    half = ROPE_DIM // 2
    inv_freq = ROPE_THETA ** (-jnp.arange(half, dtype=jnp.float32) / half)
    ang = positions.astype(jnp.float32)[:, None] * inv_freq[None, :]
    cos = jnp.cos(ang)[None, :, None, :]
    sin = jnp.sin(ang)[None, :, None, :]
    tf = t.astype(jnp.float32)
    x1 = tf[..., :half]
    x2 = tf[..., half:ROPE_DIM]
    return jnp.concatenate([x1 * cos - x2 * sin, x2 * cos + x1 * sin, tf[..., ROPE_DIM:]], axis=-1)

def gla_direction(q, k, v, log_a, include_diag):
    Bsz, H, S, dk = q.shape
    dv = v.shape[-1]
    C = GLA_CHUNK
    N = S // C
    q = q.reshape(Bsz, H, N, C, dk)
    k = k.reshape(Bsz, H, N, C, dk)
    v = v.reshape(Bsz, H, N, C, dv)
    b = jnp.cumsum(log_a.reshape(Bsz, H, N, C, dk), axis=3)
    b_last = b[:, :, :, -1:, :]
    q_in = q * jnp.exp(b)
    k_in = k * jnp.exp(-b)
    scores = jnp.einsum('bhnik,bhnjk->bhnij', q_in, k_in)
    mask = jnp.tril(jnp.ones((C, C), dtype=bool), k=0 if include_diag else -1)
    o_intra = jnp.einsum('bhnij,bhnjv->bhniv', jnp.where(mask, scores, 0.0), v)
    k_state = k * jnp.exp(b_last - b)
    inc = jnp.einsum('bhnjk,bhnjv->bhnkv', k_state, v)
    decay = jnp.exp(b_last[:, :, :, 0, :])

    def step(state, inp):
        dec, add = inp
        return dec[..., None] * state + add, state

    s0 = jnp.zeros((Bsz, H, dk, dv), jnp.float32)
    _, s_before = lax.scan(step, s0, (jnp.moveaxis(decay, 2, 0), jnp.moveaxis(inc, 2, 0)))
    s_before = jnp.moveaxis(s_before, 0, 2)
    o_inter = jnp.einsum('bhnik,bhnkv->bhniv', q_in, s_before)
    return (o_intra + o_inter).reshape(Bsz, H, S, dv)

def gla_mixer(q, k, v, gate_down_f, gate_down_b, r, up_f, bias_f, up_b, bias_b, out_g):
    Bsz, S, _ = q.shape
    f32 = jnp.float32

    def heads(t, d):
        return t.astype(f32).reshape(Bsz, S, GLA_HEADS, d).transpose(0, 2, 1, 3)

    qh = heads(q, GLA_DK) * (GLA_DK ** -0.5)
    kh = heads(k, GLA_DK)
    vh = heads(v, GLA_DV)
    la_f = heads(jax.nn.log_sigmoid(gate_down_f.astype(f32) @ up_f.astype(f32) + bias_f.astype(f32)) / GLA_TAU, GLA_DK)
    la_b = heads(jax.nn.log_sigmoid(gate_down_b.astype(f32) @ up_b.astype(f32) + bias_b.astype(f32)) / GLA_TAU, GLA_DK)

    def rev(t):
        return jnp.flip(t, axis=2)

    o_fwd = gla_direction(qh, kh, vh, la_f, True)
    o_bwd = rev(gla_direction(rev(qh), rev(kh), rev(vh), rev(la_b), False))
    o = (o_fwd + o_bwd).transpose(0, 2, 1, 3)
    o = rms_norm(o, out_g.reshape(GLA_HEADS, GLA_DV))
    return o.reshape(Bsz, S, GLA_V_W) * jax.nn.silu(r.astype(f32))

def dilated_window_attention(q, k, v, window, dilation):
    Bsz, S, H, hd = q.shape
    half = window // (2 * dilation)
    L = S // dilation
    nb = -(-L // half)
    Lp = nb * half

    def to_blocks(t):
        t = t.reshape(Bsz, L, dilation, H, hd)
        t = jnp.pad(t, ((0, 0), (0, Lp - L), (0, 0), (0, 0), (0, 0)))
        return t.reshape(Bsz, nb, half, dilation, H, hd)

    def with_neighbours(t):
        tp = jnp.pad(t, ((0, 0), (1, 1), (0, 0), (0, 0), (0, 0), (0, 0)))
        return jnp.concatenate([tp[:, :-2], tp[:, 1:-1], tp[:, 2:]], axis=2)

    qb = to_blocks(q)
    kn = with_neighbours(to_blocks(k))
    vn = with_neighbours(to_blocks(v))
    s = jnp.einsum('bnqrhe,bnkrhe->bnrhqk', qb, kn)
    qpos = jnp.arange(nb)[:, None] * half + jnp.arange(half)[None, :]
    kpos = jnp.arange(nb)[:, None] * half - half + jnp.arange(3 * half)[None, :]
    rel = kpos[:, None, :] - qpos[:, :, None]
    valid = (jnp.abs(rel) <= half) & (kpos[:, None, :] >= 0) & (kpos[:, None, :] < L)
    s = jnp.where(valid[None, :, None, None], s, MASK_VALUE)
    m = jnp.max(s, axis=-1)
    p = jnp.exp(s - m[..., None])
    den = jnp.sum(p, axis=-1)
    m_t = jnp.moveaxis(m, (2, 3, 4), (3, 4, 2))
    den_t = jnp.moveaxis(den, (2, 3, 4), (3, 4, 2))
    o = jnp.einsum('bnrhqk,bnkrhe->bnqrhe', p, vn) / den_t[..., None]

    def back(t):
        t = t.reshape((Bsz, Lp, dilation, H) + t.shape[5:])[:, :L]
        return t.reshape((Bsz, S, H) + t.shape[4:])

    return back(o), back(m_t), back(den_t)

def dilated_mixer(q, k, v, q_norm_g, k_norm_g, positions):
    Bsz, S, _ = q.shape
    shp = (Bsz, S, DIL_HEADS, HEAD_DIM)
    qh = partial_rope(rms_norm(q.reshape(shp), q_norm_g), positions) * (HEAD_DIM ** -0.5)
    kh = partial_rope(rms_norm(k.reshape(shp), k_norm_g), positions)
    vh = v.reshape(shp).astype(jnp.float32)
    outs, maxes, dens = [], [], []
    for window, dilation in DIL_PATTERNS:
        o, m, d = dilated_window_attention(qh, kh, vh, window, dilation)
        outs.append(o)
        maxes.append(m)
        dens.append(d)
    m_all = jnp.stack(maxes)
    w = jnp.stack(dens) * jnp.exp(m_all - jnp.max(m_all, axis=0, keepdims=True))
    w = w / jnp.sum(w, axis=0, keepdims=True)
    o = jnp.sum(w[..., None] * jnp.stack(outs), axis=0)
    return o.reshape(Bsz, S, DIL_W)

def peer_ffn(xn, w_query, sub_keys, expert_down, expert_up):
    Bsz, S, D = xn.shape
    f32 = jnp.float32
    T = Bsz * S
    xt = xn.reshape(T, D)
    qry = (xt @ w_query).reshape(T, PEER_HEADS, 2, PEER_QDIM // 2)
    sc = jnp.einsum('thcd,hckd->thck', qry.astype(f32), sub_keys.astype(f32))
    top_s, top_i = lax.top_k(sc, PEER_TOPK)
    kk = PEER_TOPK * PEER_TOPK
    cand_s = (top_s[:, :, 0, :, None] + top_s[:, :, 1, None, :]).reshape(T, PEER_HEADS, kk)
    cand_i = (top_i[:, :, 0, :, None] * PEER_NKEYS + top_i[:, :, 1, None, :]).reshape(T, PEER_HEADS, kk)
    best_s, best_pos = lax.top_k(cand_s, PEER_TOPK)
    idx = jnp.take_along_axis(cand_i, best_pos, axis=-1)
    gates = jax.nn.softmax(best_s, axis=-1)
    K = PEER_HEADS * PEER_TOPK
    nblk = T // PEER_TOKEN_BLOCK

    def block(args):
        xb, ib, gb = args
        u = expert_down[ib]
        act = jax.nn.gelu(jnp.einsum('tkd,td->tk', u, xb).astype(f32))
        vv = expert_up[ib]
        return jnp.einsum('tk,tkd->td', (gb * act).astype(vv.dtype), vv)

    out = lax.map(block, (xt.reshape(nblk, PEER_TOKEN_BLOCK, D),
                          idx.reshape(nblk, PEER_TOKEN_BLOCK, K),
                          gates.reshape(nblk, PEER_TOKEN_BLOCK, K)))
    return out.reshape(Bsz, S, D).astype(xn.dtype)

def first_inputs(seed: int = 0) -> dict:
    key = jax.random.key(seed)
    ks = jax.random.split(key, 16)
    f32 = jnp.float32

    def nrm(k, shape, scale):
        return jax.random.normal(k, shape, f32) * scale

    def gain(k, shape):
        return 1.0 + 0.02 * jax.random.normal(k, shape, f32)

    L = DEPTH
    return {
        'x': nrm(ks[0], (BATCH, SEQ, D_MODEL), 1.0),
        'norm1_g': gain(ks[1], (L, D_MODEL)),
        'w_in': nrm(ks[2], (L, D_MODEL, IN_W), D_MODEL ** -0.5),
        'gla_up_f': nrm(ks[3], (L, GLA_GATE_RANK, GLA_QK_W), GLA_GATE_RANK ** -0.5),
        'gla_bias_f': nrm(ks[4], (L, GLA_QK_W), 0.1),
        'gla_up_b': nrm(ks[5], (L, GLA_GATE_RANK, GLA_QK_W), GLA_GATE_RANK ** -0.5),
        'gla_bias_b': nrm(ks[6], (L, GLA_QK_W), 0.1),
        'gla_out_g': gain(ks[7], (L, GLA_V_W)),
        'q_norm_g': gain(ks[8], (L, HEAD_DIM)),
        'k_norm_g': gain(ks[9], (L, HEAD_DIM)),
        'w_out': nrm(ks[10], (L, MIX_W, D_MODEL), MIX_W ** -0.5),
        'norm2_g': gain(ks[11], (L, D_MODEL)),
        'peer_w_query': nrm(ks[12], (L, D_MODEL, PEER_HEADS * PEER_QDIM), D_MODEL ** -0.5),
        'peer_sub_keys': nrm(ks[13], (L, PEER_HEADS, 2, PEER_NKEYS, PEER_QDIM // 2), (PEER_QDIM // 2) ** -0.5),
        'peer_down': nrm(ks[14], (L, PEER_NEXPERTS, D_MODEL), D_MODEL ** -0.5),
        'peer_up': nrm(ks[15], (L, PEER_NEXPERTS, D_MODEL), PEER_HEADS ** -0.5),
    }

def first_block(x, norm1_g, w_in, gla_up_f, gla_bias_f, gla_up_b, gla_bias_b, gla_out_g, q_norm_g, k_norm_g, w_out, norm2_g, peer_w_query, peer_sub_keys, peer_down, peer_up):
    positions = jnp.arange(x.shape[1], dtype=jnp.int32)
    split_points = [int(c) for c in np.cumsum(IN_SPLITS)[:-1]]
    for l in range(DEPTH):
        xn = rms_norm(x, norm1_g[l])
        h = xn @ w_in[l]
        qa, ka, va, gdf, gdb, ra, qd, kd, vd = jnp.split(h, split_points, axis=-1)
        oa = gla_mixer(qa, ka, va, gdf, gdb, ra, gla_up_f[l], gla_bias_f[l], gla_up_b[l], gla_bias_b[l], gla_out_g[l])
        od = dilated_mixer(qd, kd, vd, q_norm_g[l], k_norm_g[l], positions)
        mixed = jnp.concatenate([oa, od], axis=-1).astype(x.dtype)
        x = x + mixed @ w_out[l]
        x = x + peer_ffn(rms_norm(x, norm2_g[l]), peer_w_query[l], peer_sub_keys[l], peer_down[l], peer_up[l])
    return x


MEM_LEN = 256
MIX_W_2 = D_MODEL
LRU_W = MIX_W_2 // 4
LRU_BLOCKS = 4
LRU_CONV = 4
LRU_C = 8.0
ML_W = 3 * MIX_W_2 // 8
ML_HEADS = 4
ML_DH = ML_W // ML_HEADS
ML_QKV_BLOCK = 4
ML_CONV = 4
ML_CHUNK = 128
MO_W = MIX_W_2 - LRU_W - ML_W
MO_HEADS = 6
MO_DH = MO_W // MO_HEADS
MOBA_BLOCK = 256
MOBA_TOPK = 3
MOBA_Q_CHUNK = 16
XA_HEADS = 4
XA_DH = 128
XA_W = XA_HEADS * XA_DH

RMS_EPS = 1e-6
LN_EPS = 1e-5
NEG_INF = -1e30

SPLIT_SIZES = (LRU_W, LRU_W, ML_W, ML_W, ML_W, ML_HEADS, ML_HEADS, MO_W, MO_W, MO_W, MO_W)
IN_COLS = sum(SPLIT_SIZES)
SPLIT_POINTS = tuple(int(v) for v in np.cumsum(SPLIT_SIZES)[:-1])


def rms_norm_2(x, g):
    x32 = x.astype(jnp.float32)
    y = x32 * lax.rsqrt(jnp.mean(x32 * x32, axis=-1, keepdims=True) + RMS_EPS)
    return (y * g.astype(jnp.float32)).astype(x.dtype)

def causal_conv(x, w, b):
    K = w.shape[0]
    T = x.shape[1]
    xp = jnp.pad(x, ((0, 0), (K - 1, 0), (0, 0)))
    return sum(xp[:, j:j + T] * w[j] for j in range(K)) + b

def block_diag(x, w):
    G, bi, bo = w.shape
    xs = x.reshape(x.shape[:-1] + (G, bi))
    return jnp.einsum('...gi,gio->...go', xs, w).reshape(x.shape[:-1] + (G * bo,))

def alibi_slopes(n):
    def pow2(m):
        start = 2.0 ** (-8.0 / m)
        return [start ** (i + 1) for i in range(m)]
    if math.log2(n).is_integer():
        s = pow2(n)
    else:
        c = 2 ** int(math.floor(math.log2(n)))
        s = pow2(c) + pow2(2 * c)[0::2][:n - c]
    return jnp.array(s, dtype=jnp.float32)

def rg_lru_branch(xb, zb, conv_w, conv_b, wa, ba, wx, bx, lam):
    xc = causal_conv(xb, conv_w, conv_b).astype(jnp.float32)
    r = jax.nn.sigmoid(block_diag(xc, wa) + ba)
    i = jax.nn.sigmoid(block_diag(xc, wx) + bx)
    log_a = -LRU_C * r * jax.nn.softplus(-lam.astype(jnp.float32))
    a = jnp.exp(log_a)
    u = jnp.sqrt(-jnp.expm1(2.0 * log_a)) * (i * xc)

    def combine(left, right):
        a1, b1 = left
        a2, b2 = right
        return a1 * a2, a2 * b1 + b2

    _, h = lax.associative_scan(combine, (a, u), axis=1)
    return (h * jax.nn.silu(zb.astype(jnp.float32))).astype(xb.dtype)

def mlstm_chunkwise(q, k, v, ig, lf):
    B, H, T, dh = q.shape
    L = ML_CHUNK
    nc = T // L
    q, k, v = (t.reshape(B, H, nc, L, dh) for t in (q, k, v))
    ig = ig.reshape(B, H, nc, L)
    lf = lf.reshape(B, H, nc, L)
    b = jnp.cumsum(lf, axis=-1)
    g = b[..., -1]
    a = g[..., None] - b + ig
    m_loc = jnp.max(a, axis=-1)
    w = jnp.exp(a - m_loc[..., None])
    c_loc = jnp.einsum('bhcl,bhcld,bhcle->bhcde', w, k, v)
    n_loc = jnp.einsum('bhcl,bhcld->bhcd', w, k)

    def step(carry, inp):
        c_st, n_st, m_st = carry
        c_l, n_l, m_l, g_c = inp
        m_new = jnp.maximum(g_c + m_st, m_l)
        s_old = jnp.exp(g_c + m_st - m_new)
        s_new = jnp.exp(m_l - m_new)
        c_new = s_old[..., None, None] * c_st + s_new[..., None, None] * c_l
        n_new = s_old[..., None] * n_st + s_new[..., None] * n_l
        return (c_new, n_new, m_new), (c_st, n_st, m_st)

    init = (jnp.zeros((B, H, dh, dh), jnp.float32), jnp.zeros((B, H, dh), jnp.float32),
            jnp.zeros((B, H), jnp.float32))
    xs = tuple(jnp.moveaxis(t, 2, 0) for t in (c_loc, n_loc, m_loc, g))
    _, (c_prev, n_prev, m_prev) = lax.scan(step, init, xs)
    c_prev = jnp.moveaxis(c_prev, 0, 2)
    n_prev = jnp.moveaxis(n_prev, 0, 2)
    m_prev = jnp.moveaxis(m_prev, 0, 2)
    causal = jnp.tril(jnp.ones((L, L), dtype=bool))
    d = jnp.where(causal, b[..., :, None] - b[..., None, :] + ig[..., None, :], -jnp.inf)
    inter = b + m_prev[..., None]
    m = jnp.maximum(inter, jnp.max(d, axis=-1))
    s = jnp.einsum('bhcjd,bhcsd->bhcjs', q, k) * jnp.exp(d - m[..., None])
    s_int = jnp.exp(inter - m)
    num = (jnp.einsum('bhcjs,bhcsd->bhcjd', s, v)
           + s_int[..., None] * jnp.einsum('bhcjd,bhcde->bhcje', q, c_prev))
    den = jnp.sum(s, axis=-1) + s_int * jnp.einsum('bhcjd,bhcd->bhcj', q, n_prev)
    h = num / jnp.maximum(jnp.abs(den), jnp.exp(-m))[..., None]
    return h.reshape(B, H, T, dh)

def mlstm_branch(u, o, z, ig_pre, fg_pre, conv_w, conv_b, wq, wk, wv, bi, bf, norm_g):
    B, T, _ = u.shape
    uc = jax.nn.silu(causal_conv(u, conv_w, conv_b))
    q = block_diag(uc, wq)
    k = block_diag(uc, wk) * (ML_DH ** -0.5)
    v = block_diag(u, wv)

    def heads(t):
        return t.astype(jnp.float32).reshape(B, T, ML_HEADS, ML_DH).transpose(0, 2, 1, 3)

    ig = (ig_pre.astype(jnp.float32) + bi).transpose(0, 2, 1)
    lf = jax.nn.log_sigmoid(fg_pre.astype(jnp.float32) + bf).transpose(0, 2, 1)
    h = mlstm_chunkwise(heads(q), heads(k), heads(v), ig, lf).transpose(0, 2, 1, 3)
    h = jax.nn.sigmoid(o.astype(jnp.float32)).reshape(B, T, ML_HEADS, ML_DH) * h
    mu = jnp.mean(h, axis=-1, keepdims=True)
    var = jnp.mean(jnp.square(h - mu), axis=-1, keepdims=True)
    hn = (h - mu) * lax.rsqrt(var + LN_EPS) * norm_g.astype(jnp.float32).reshape(ML_HEADS, ML_DH)
    return (hn.reshape(B, T, ML_W) * jax.nn.silu(z.astype(jnp.float32))).astype(u.dtype)

def moba_attention(q, k, v):
    B, H, T, dh = q.shape
    nb = -(-T // MOBA_BLOCK)
    tp = nb * MOBA_BLOCK
    pad = ((0, 0), (0, 0), (0, tp - T), (0, 0))
    q, k, v = (jnp.pad(t, pad) for t in (q, k, v))
    kb = k.reshape(B, H, nb, MOBA_BLOCK, dh)
    vb = v.reshape(B, H, nb, MOBA_BLOCK, dh)
    kmean = jnp.mean(kb.astype(jnp.float32), axis=3)
    n_sel = min(MOBA_TOPK, nb - 1)
    slopes = alibi_slopes(H)
    scale = dh ** -0.5
    nq = tp // MOBA_Q_CHUNK
    qc = jnp.moveaxis(q.reshape(B, H, nq, MOBA_Q_CHUNK, dh), 2, 0)
    bidx = jnp.arange(B)[:, None, None, None]
    hidx = jnp.arange(H)[None, :, None, None]
    s_local = jnp.arange(MOBA_BLOCK)

    def one_chunk(args):
        qch, ci = args
        qch = qch.astype(jnp.float32)
        t = ci * MOBA_Q_CHUNK + jnp.arange(MOBA_Q_CHUNK)
        bq = (ci * MOBA_Q_CHUNK) // MOBA_BLOCK
        k_own = lax.dynamic_index_in_dim(kb, bq, axis=2, keepdims=False).astype(jnp.float32)
        v_own = lax.dynamic_index_in_dim(vb, bq, axis=2, keepdims=False).astype(jnp.float32)
        dist_own = (t[:, None] - (bq * MOBA_BLOCK + s_local)[None, :]).astype(jnp.float32)
        l_own = jnp.einsum('bhqd,bhsd->bhqs', qch, k_own) * scale - slopes[:, None, None] * dist_own
        l_own = jnp.where(dist_own >= 0, l_own, NEG_INF)
        if n_sel == 0:
            p_own = jax.nn.softmax(l_own, axis=-1)
            return jnp.einsum('bhqs,bhsd->bhqd', p_own, v_own)
        gate = jnp.einsum('bhqd,bhnd->bhqn', qch, kmean)
        gate = jnp.where(jnp.arange(nb) < bq, gate, -jnp.inf)
        _, idx = lax.top_k(gate, n_sel)
        k_sel = kb[bidx, hidx, idx].astype(jnp.float32)
        v_sel = vb[bidx, hidx, idx].astype(jnp.float32)
        dist_sel = (t[:, None, None] - (idx[..., None] * MOBA_BLOCK + s_local)).astype(jnp.float32)
        l_sel = (jnp.einsum('bhqd,bhqnsd->bhqns', qch, k_sel) * scale
                 - slopes[:, None, None, None] * dist_sel)
        l_sel = jnp.where((jnp.arange(n_sel) < bq)[:, None], l_sel, NEG_INF)
        n_past = n_sel * MOBA_BLOCK
        logits = jnp.concatenate(
            [l_sel.reshape(B, H, MOBA_Q_CHUNK, n_past), l_own], axis=-1)
        p = jax.nn.softmax(logits, axis=-1)
        p_sel = p[..., :n_past].reshape(B, H, MOBA_Q_CHUNK, n_sel, MOBA_BLOCK)
        p_own = p[..., n_past:]
        return (jnp.einsum('bhqns,bhqnsd->bhqd', p_sel, v_sel)
                + jnp.einsum('bhqs,bhsd->bhqd', p_own, v_own))

    out = lax.map(one_chunk, (qc, jnp.arange(nq)))
    out = jnp.moveaxis(out, 0, 2).reshape(B, H, tp, dh)
    return out[:, :, :T]

def moba_branch(qb, kb, vb, zb):
    B, T, _ = qb.shape

    def heads(t):
        return t.reshape(B, T, MO_HEADS, MO_DH).transpose(0, 2, 1, 3)

    o = moba_attention(heads(qb), heads(kb), heads(vb)).transpose(0, 2, 1, 3).reshape(B, T, MO_W)
    return (o * jax.nn.silu(zb.astype(jnp.float32))).astype(qb.dtype)

def memory_cross_attention(h, mem_n, wq, wkv, wo):
    B, T, _ = h.shape
    M = mem_n.shape[1]
    q = (h @ wq).reshape(B, T, XA_HEADS, XA_DH)
    k, v = jnp.split(mem_n @ wkv, 2, axis=-1)
    k = k.reshape(B, M, XA_HEADS, XA_DH)
    v = v.reshape(B, M, XA_HEADS, XA_DH)
    s = jnp.einsum('bthd,bmhd->bhtm', q, k).astype(jnp.float32) * (XA_DH ** -0.5)
    p = jax.nn.softmax(s, axis=-1).astype(v.dtype)
    o = jnp.einsum('bhtm,bmhd->bthd', p, v).reshape(B, T, XA_W)
    return o @ wo

def second_inputs(seed: int = 0) -> dict:
    key = jax.random.key(seed)
    ks = jax.random.split(key, 26)

    def nrm(k, shape, scale):
        return scale * jax.random.normal(k, shape, jnp.float32)

    def gain(k, shape):
        return 1.0 + 0.02 * jax.random.normal(k, shape, jnp.float32)

    u = jax.random.uniform(ks[10], (DEPTH, LRU_W), jnp.float32, 0.9, 0.999)
    a = u ** (1.0 / LRU_C)
    lam = jnp.log(a) - jnp.log1p(-a)
    bl = LRU_W // LRU_BLOCKS
    nqkv = ML_W // ML_QKV_BLOCK
    return {
        "x": nrm(ks[0], (BATCH, SEQ, D_MODEL), 1.0),
        "mem": nrm(ks[1], (BATCH, MEM_LEN, D_MODEL), 1.0),
        "mix_norm_g": gain(ks[2], (DEPTH, D_MODEL)),
        "w_in": nrm(ks[3], (DEPTH, D_MODEL, IN_COLS), D_MODEL ** -0.5),
        "lru_conv_w": nrm(ks[4], (DEPTH, LRU_CONV, LRU_W), LRU_CONV ** -0.5),
        "lru_conv_b": nrm(ks[5], (DEPTH, LRU_W), 0.02),
        "lru_wa": nrm(ks[6], (DEPTH, LRU_BLOCKS, bl, bl), bl ** -0.5),
        "lru_ba": nrm(ks[7], (DEPTH, LRU_W), 0.02),
        "lru_wx": nrm(ks[8], (DEPTH, LRU_BLOCKS, bl, bl), bl ** -0.5),
        "lru_bx": nrm(ks[9], (DEPTH, LRU_W), 0.02),
        "lru_lambda": lam,
        "ml_conv_w": nrm(ks[11], (DEPTH, ML_CONV, ML_W), ML_CONV ** -0.5),
        "ml_conv_b": nrm(ks[12], (DEPTH, ML_W), 0.02),
        "ml_wq": nrm(ks[13], (DEPTH, nqkv, ML_QKV_BLOCK, ML_QKV_BLOCK), ML_QKV_BLOCK ** -0.5),
        "ml_wk": nrm(ks[14], (DEPTH, nqkv, ML_QKV_BLOCK, ML_QKV_BLOCK), ML_QKV_BLOCK ** -0.5),
        "ml_wv": nrm(ks[15], (DEPTH, nqkv, ML_QKV_BLOCK, ML_QKV_BLOCK), ML_QKV_BLOCK ** -0.5),
        "ml_bi": nrm(ks[16], (DEPTH, ML_HEADS), 0.1),
        "ml_bf": jnp.linspace(3.0, 6.0, ML_HEADS, dtype=jnp.float32)[None, :] + nrm(ks[17], (DEPTH, ML_HEADS), 0.02),
        "ml_norm_g": gain(ks[18], (DEPTH, ML_W)),
        "w_out": nrm(ks[19], (DEPTH, MIX_W_2, D_MODEL), MIX_W_2 ** -0.5),
        "xa_norm_g": gain(ks[20], (DEPTH, D_MODEL)),
        "mem_norm_g": gain(ks[21], (DEPTH, D_MODEL)),
        "xa_wq": nrm(ks[22], (DEPTH, D_MODEL, XA_W), D_MODEL ** -0.5),
        "xa_wkv": nrm(ks[23], (DEPTH, D_MODEL, 2 * XA_W), D_MODEL ** -0.5),
        "xa_wo": nrm(ks[24], (DEPTH, XA_W, D_MODEL), XA_W ** -0.5),
        "final_norm_g": gain(ks[25], (D_MODEL,)),
    }

def second_block(x, mem, mix_norm_g, w_in, lru_conv_w, lru_conv_b, lru_wa, lru_ba, lru_wx, lru_bx,
              lru_lambda, ml_conv_w, ml_conv_b, ml_wq, ml_wk, ml_wv, ml_bi, ml_bf, ml_norm_g,
              w_out, xa_norm_g, mem_norm_g, xa_wq, xa_wkv, xa_wo, final_norm_g):
    for l in range(DEPTH):
        h = rms_norm_2(x, mix_norm_g[l])
        p = h @ w_in[l]
        (lru_x, lru_z, ml_u, ml_o, ml_z, ml_i, ml_f,
         mo_q, mo_k, mo_v, mo_z) = jnp.split(p, SPLIT_POINTS, axis=-1)
        y_lru = rg_lru_branch(lru_x, lru_z, lru_conv_w[l], lru_conv_b[l], lru_wa[l], lru_ba[l],
                              lru_wx[l], lru_bx[l], lru_lambda[l])
        y_ml = mlstm_branch(ml_u, ml_o, ml_z, ml_i, ml_f, ml_conv_w[l], ml_conv_b[l], ml_wq[l],
                            ml_wk[l], ml_wv[l], ml_bi[l], ml_bf[l], ml_norm_g[l])
        y_mo = moba_branch(mo_q, mo_k, mo_v, mo_z)
        y = jnp.concatenate([y_lru, y_ml, y_mo], axis=-1)
        x = x + y @ w_out[l]
        hx = rms_norm_2(x, xa_norm_g[l])
        hm = rms_norm_2(mem, mem_norm_g[l])
        x = x + memory_cross_attention(hx, hm, xa_wq[l], xa_wkv[l], xa_wo[l])
    return rms_norm_2(x, final_norm_g)


def setup_inputs(seed=0):
    out = dict(first_inputs(seed))
    for name, value in second_inputs(seed + 1).items():
        if name != "x":
            out[name + "_2"] = value
    return out


def reference(
    x, norm1_g, w_in, gla_up_f, gla_bias_f, gla_up_b, gla_bias_b, gla_out_g, q_norm_g, k_norm_g,
    w_out, norm2_g, peer_w_query, peer_sub_keys, peer_down, peer_up, mem_2, mix_norm_g_2,
    w_in_2, lru_conv_w_2, lru_conv_b_2, lru_wa_2, lru_ba_2, lru_wx_2, lru_bx_2, lru_lambda_2,
    ml_conv_w_2, ml_conv_b_2, ml_wq_2, ml_wk_2, ml_wv_2, ml_bi_2, ml_bf_2, ml_norm_g_2, w_out_2,
    xa_norm_g_2, mem_norm_g_2, xa_wq_2, xa_wkv_2, xa_wo_2, final_norm_g_2,
):
    x = first_block(
        x, norm1_g, w_in, gla_up_f, gla_bias_f, gla_up_b, gla_bias_b, gla_out_g, q_norm_g,
        k_norm_g, w_out, norm2_g, peer_w_query, peer_sub_keys, peer_down, peer_up,
    )
    return second_block(
        x, mem_2, mix_norm_g_2, w_in_2, lru_conv_w_2, lru_conv_b_2, lru_wa_2, lru_ba_2,
        lru_wx_2, lru_bx_2, lru_lambda_2, ml_conv_w_2, ml_conv_b_2, ml_wq_2, ml_wk_2, ml_wv_2,
        ml_bi_2, ml_bf_2, ml_norm_g_2, w_out_2, xa_norm_g_2, mem_norm_g_2, xa_wq_2, xa_wkv_2,
        xa_wo_2, final_norm_g_2,
    )


_drawn_inputs = setup_inputs


def setup_inputs(seed=0):
    import zlib

    import numpy as np

    out = dict(_drawn_inputs(seed))
    spreads = {}
    factors = {'gla_bias_f': 2.737,
     'gla_out_g': 3.418,
     'q_norm_g': 5.546,
     'k_norm_g': 5.154,
     'mix_norm_g_2': 2.759,
     'lru_conv_b_2': 2.798,
     'lru_ba_2': 23.104,
     'lru_bx_2': 8.0,
     'ml_conv_b_2': 5.744,
     'ml_bi_2': 64.0,
     'ml_norm_g_2': 8.0,
     'xa_norm_g_2': 8.0,
     'mem_norm_g_2': 8.0,
     'final_norm_g_2': 7.48}
    for name, (base, spread) in spreads.items():
        noise = np.random.default_rng([zlib.crc32(name.encode()), seed]).standard_normal(out[name].shape)
        drawn = base * np.exp(spread * noise) if base else spread * noise
        out[name] = jnp.asarray(drawn.astype(out[name].dtype))
    for name, factor in factors.items():
        out[name] = (out[name] * factor).astype(out[name].dtype)
    return out
```

```python
from contextlib import ExitStack

import numpy as np

import concourse.bass as bass
from concourse import mybir

F32 = mybir.dt.float32
F32R = mybir.dt.float32r
U32 = mybir.dt.uint32
I32 = mybir.dt.int32
ALU = mybir.AluOpType
ACT = mybir.ActivationFunctionType
AX = mybir.AxisListType

P = 128
D = 2048
T = 256
NT = T // P
KC = D // P
EPS = 1e-6
LN_EPS = 1e-5
NEG = -1e30

GLA_H, GLA_DK, GLA_DV, GLA_RANK, GLA_CHUNK, GLA_TAU = 4, 64, 128, 16, 64, 16.0
DIL_H, HD = 12, 128
ROPE = 32
HALF = ROPE // 2
PATTERNS = ((128, 1), (512, 4), (2048, 16))
PEER_H, PEER_K, PEER_TOP = 8, 128, 16
LRU_W, ML_W, MO_W = 512, 768, 768
ML_H, ML_DH, ML_C = 4, 192, 96
MLC = ML_W // ML_C
MO_H, XA_H = 6, 4
TAPS = 4

SLOT = 4 * 512
NSLOT = 8

H_QA, H_KA, H_VA, H_RA, H_QD, H_KD, H_VD = 0, 256, 512, 1024, 1536, 3072, 4608
H_W = 6144


def chunk_masks():
    j, i = np.arange(P)[:, None], np.arange(P)[None, :]
    same = (j // GLA_CHUNK) == (i // GLA_CHUNK)
    c = {}
    c["ident"] = (j == i).astype(np.float32)
    c["ones"] = np.ones((P, P), np.float32)
    c["tri_f"] = (same & (j <= i)) / GLA_TAU
    c["tri_b"] = (same & (j >= i)) / GLA_TAU
    c["same"] = same / GLA_TAU
    c["half"] = (np.arange(P)[:, None] // GLA_CHUNK == np.arange(2)[None, :]) / GLA_TAU
    c["keep_f"] = np.tile((same & (j <= i)).astype(np.float32)[:, None, :], (1, GLA_H, 1))
    c["keep_b"] = np.tile((same & (j > i)).astype(np.float32)[:, None, :], (1, GLA_H, 1))
    c["tri"] = (j <= i).astype(np.float32)
    c["causal"] = np.tile(np.where(i <= j, 0.0, NEG)[:, None, :], (1, ML_H, 1))
    q, k = np.arange(T)[:, None], np.arange(T)[None, :]
    count = sum(((np.abs(q // d - k // d) <= w // (2 * d)) & (q % d == k % d)).astype(int) for w, d in PATTERNS)
    logc = np.where(count > 0, np.log(np.maximum(count, 1)), NEG)
    c["logc"] = logc.reshape(NT, P, T).transpose(1, 0, 2)
    freq = 500000.0 ** (-np.arange(HALF, dtype=np.float32) / np.float32(HALF))
    ang = np.arange(T, dtype=np.float32)[:, None] * freq.astype(np.float32)[None, :]
    c["cos"] = np.cos(ang).reshape(NT, P, HALF).transpose(1, 0, 2)
    c["sin"] = np.sin(ang).reshape(NT, P, HALF).transpose(1, 0, 2)
    g = np.arange(ML_C)[:, None] // 4 == np.arange(ML_C // 4)[None, :]
    c["group"] = np.pad(g.astype(np.float32), ((0, P - ML_C), (0, 0)))
    c["iota"] = np.tile(np.arange(PEER_TOP, dtype=np.float32)[None, :], (P, 1))
    return {n: np.ascontiguousarray(a, dtype=np.float32).reshape(P, -1) for n, a in c.items()}


def alibi_bias():
    slopes = [2.0 ** (-8.0 / 4 * (i + 1)) for i in range(4)] + [2.0 ** (-8.0 / 8 * (i + 1)) for i in (0, 2)]
    dist = (np.arange(T)[:, None] - np.arange(T)[None, :]).astype(np.float32)
    b = np.stack([np.where(dist >= 0, -np.float32(s) * dist, NEG) for s in slopes])
    return np.ascontiguousarray(b.reshape(MO_H, NT, P, T).transpose(2, 0, 1, 3), dtype=np.float32).reshape(P, -1)


def pack(parts):
    at, n = {}, 0
    for name, a in parts.items():
        at[name] = (n, a.shape[1])
        n += a.shape[1]
    return np.ascontiguousarray(np.concatenate(list(parts.values()), axis=1)), at


def shaped(ap, *dims):
    if len(dims) == 1:
        return ap
    names = "abcd"[:len(dims)]
    return ap.rearrange(f"p ({' '.join(names)}) -> p {' '.join(names)}", **dict(zip(names, dims)))


class Area:

    def __init__(self, *aps):
        self.aps = list(aps)
        self.used = [0] * len(aps)

    def take(self, *dims, parts=P):
        n = int(np.prod(dims))
        for i, ap in enumerate(self.aps):
            if self.used[i] + n <= ap.shape[1]:
                at = self.used[i]
                self.used[i] += n
                return shaped(ap[0:parts, at:at + n], *dims)
        raise ValueError(f"no room for {dims}")


class Chain:

    def __init__(self, eng, sem, count=0):
        self.eng, self.sem, self.count = eng, sem, count

    def __call__(self, ins):
        self.count += 1
        ins.then_inc(self.sem, 1)
        self.eng.wait_ge(self.sem, self.count)


def repeat(eng, n, body):
    body(0, True)
    if n > 1:
        with eng.Fori(1, n) as i:
            body(i, False)


class Job:

    def __init__(self, w, kind, act_t, dest, m=P, add=None, unroll=2):
        self.w, self.kind, self.act_t, self.dest, self.m, self.add = w, kind, act_t, dest, m, add
        self.blocks, _, self.kc, self.cols = w.shape
        self.groups = NT if kind == "tok" else self.cols // m
        self.unroll = unroll if self.blocks % 2 == 0 else 1
        if kind == "fold":
            self.groups = NT * 4
        self.started = 0


class Program:
    def __init__(self, nc, ctx, ins, out, where):
        self.nc, self.ctx, self.ins, self.out, self.where = nc, ctx, ins, out, where
        self.block0 = 0
        self.groups_after = []
        self.evac0 = 0
        n_const = ins["consts"].shape[1]
        self.ring = self.sb("ring", NSLOT * SLOT)
        self.ring_r = self.rounded("ring_r", NSLOT * SLOT)
        self.x = self.sb("x_res", NT * D)
        self.act_t = self.sb("act_t", KC * T)
        self.act_r = self.rounded("act_r", KC * T)
        self.mix_t = self.sb("mix_t", KC * T)
        self.mix_r = self.rounded("mix_r", KC * T)
        self.mem_kv = self.sb("mem_kv", 2 * XA_H * T)
        self.h = self.sb("h", 13312)
        self.const = self.sb("const", n_const)
        self.work = self.sb("work", 6144)
        self.banks = [ctx.enter_context(nc.psum_tensor(f"bank{i}", [P, 512], F32)) for i in range(8)]
        self.x3 = shaped(self.x[:, :], NT, D)
        self.act3 = shaped(self.act_t[:, :], KC, T)
        self.mix3 = shaped(self.mix_t[:, :], KC, T)
        self.slots = shaped(self.ring[:, :], NSLOT, SLOT)
        self.slots_r = shaped(self.ring_r[:, :], NSLOT, SLOT)
        self.stage_sems = []
        self.loaded = [self.lasting_sem(f"slot{i}_loaded") for i in range(4)]
        self.weights_high = self.lasting_sem("weights_high")
        self.weights_low = self.lasting_sem("weights_low")
        self.slot_used = self.lasting_sem("slot_used")
        self.group_done = self.lasting_sem("group_done")
        self.group_out = self.lasting_sem("group_out")

    def sb(self, name, n):
        return self.ctx.enter_context(self.nc.sbuf_tensor(name, [P, n], F32))

    def rounded(self, name, n):
        return self.nc.alloc_sbuf_tensor_at(name, [P, n], F32R, offset=self.nc.sbuf_base - 4 * n)

    def lasting_sem(self, name):
        return self.ctx.enter_context(self.nc.semaphore(name))

    def sem(self, name):
        self.stage_sems.append(self.nc.alloc_semaphore(name=name))
        return self.stage_sems[-1]

    def recycle(self):
        nums = sorted(s.num for s in self.stage_sems)
        starts = [n for n in nums if n - 1 not in nums]
        with self.nc.Block() as block:
            @block.gpsimd
            def _(pool):
                for a in starts:
                    b = a
                    while b in nums:
                        b += 1
                    pool.sem_clear(range(a, b))
        for s in self.stage_sems:
            self.nc.release_semaphore(s)
        self.stage_sems = []

    def c(self, name, *dims):
        at, n = self.where[name]
        return shaped(self.const[:, at:at + n], *(dims or (n,)))



CHUNKS = 4


def load_chunks(sp, k, job, b, n, groups_done):
    for s in range(CHUNKS):
        if groups_done is not None:
            if s < CHUNKS - 1:
                sp.wait_ge(k.slot_used, n * 3 + (s + 1 - 3))
            else:
                sp.wait_ge(k.group_done, groups_done)
        dst = shaped(k.slots[:, s, 0:4 * job.cols], 4, job.cols)
        src = job.w[b] if isinstance(b, int) else job.w[bass.ds(b, 1), :, :, :].rearrange("o p k c -> (o p) k c")
        sp.dma_start(dst, src[:, 4 * s:4 * s + 4, :]).then_inc(k.loaded[s], 16)


def start_stream(sp, k, job):
    n = k.block0
    load_chunks(sp, k, job, 0, n, k.groups_after[n - 1] if n >= 1 else None)
    job.started = 1


class Beside:

    def __init__(self, load, vector, scalar):
        self.load, self.vector, self.scalar = load, vector, scalar


def project(k, jobs, name, upcoming=None, beside=None):
    nc = k.nc
    starts, evacs = [], []
    n, g = k.block0, k.evac0
    for job in jobs:
        starts.append(n)
        evacs.append(g)
        for _ in range(job.blocks):
            n, g = n + 1, g + job.groups
            k.groups_after.append(g)
    after_blocks, after_groups = n, g
    in_mix = jobs[0].kind == "fold" or jobs[0].add is not None
    raw_a, low_a, high_a = (k.mix_t, k.mix_r, k.act_r) if in_mix else (k.act_t, k.act_r, k.mix_r)
    act_kc = jobs[0].kc if jobs[0].kind != "fold" else 4
    a_raw, a_hi, a_lo = (shaped(t[:, :], KC, T) for t in (raw_a, high_a, low_a))
    act_high, act_low = k.sem(name + "_act_high"), k.sem(name + "_act_low")
    plain = lambda ap: ap.bitcast(F32)

    def high(s, job):
        return k.slots_r[:, CHUNKS + s, 0:4 * job.cols]

    def low(s, job):
        return k.slots_r[:, s, 0:4 * job.cols]

    def over_blocks(eng, body):
        before = None
        for job, n0, g0 in zip(jobs, starts, evacs):
            if job.unroll == 1:
                for b in range(job.blocks):
                    g = g0 + b * job.groups
                    body(job, b, b, n0 + b, g, True, before)
                    before = (job, b, b, g)
                continue

            def turn(i, first, job=job, n0=n0, g0=g0, before=before):
                for j in range(2):
                    g = i * (2 * job.groups) + (g0 + j * job.groups)
                    if j == 1:
                        before = (job, i * 2, 0, i * (2 * job.groups) + g0)
                    elif not first:
                        before = (job, i * 2 - 1, 1, i * (2 * job.groups) + (g0 - job.groups))
                    body(job, i * 2 + j, j, i * 2 + (n0 + j), g, first, before)

            repeat(eng, job.blocks // 2, turn)
            before = (job, job.blocks - 1, 1, g0 + (job.blocks - 1) * job.groups)
        return before

    adds = jobs[0].add is not None

    def with_activations(before, s):
        return before is None and s < act_kc // 4

    def take_out(eng, job, b, j, g):
        for gi in range(job.groups):
            eng.wait_ge(k.group_done, g + (gi + 1))
            bank = k.banks[(b * job.groups + gi) % max(job.groups, 4) if job.unroll == 1 else j * job.groups + gi]
            src = bank[:, 0:job.cols] if job.kind != "feat" else bank[0:job.m, 0:T]
            if adds:
                m = eng.tensor_tensor(job.dest(b, gi), src, job.add(b, gi), ALU.add)
            else:
                m = eng.activation(job.dest(b, gi), src, ACT.Copy)
            m.then_inc(k.group_out, 1)

    with nc.Block() as block:

        @block.sync
        def _(sp):
            if beside is not None:
                beside.load(sp)
            for job, n0, g0 in zip(jobs, starts, evacs):
                straight = job.blocks if job.unroll == 1 else 2
                for b in range(job.started, straight):
                    n = n0 + b
                    load_chunks(sp, k, job, b, n, k.groups_after[n - 1] if n >= 1 else None)
                if straight < job.blocks:
                    with sp.Fori(1, job.blocks // 2) as i:
                        for j in range(2):
                            load_chunks(sp, k, job, 2 * i + j, 2 * i + (n0 + j),
                                        i * (2 * job.groups) + (g0 + j * job.groups))
            if upcoming is not None:
                k.block0 = after_blocks
                start_stream(sp, k, upcoming)

        @block.scalar
        def _(act):
            def body(job, b, j, n, g, first, before):
                if beside is not None and job is jobs[-1] and b in beside.scalar:
                    beside.scalar[b](act)
                for s in range(CHUNKS):
                    if with_activations(before, s):
                        part = slice(4 * s, 4 * s + 4)
                        act.activation(a_hi[:, part, :], a_raw[:, part, :], ACT.Copy).then_inc(act_high, 1)
                    if s == CHUNKS - 1 and before is not None and not adds:
                        take_out(act, *before)
                    act.wait_ge(k.loaded[s], n * 16 + 16)
                    act.activation(high(s, job), k.slots[:, s, 0:4 * job.cols], ACT.Copy).then_inc(k.weights_high, 1)

            last = over_blocks(act, body)
            if not adds:
                take_out(act, *last)

        @block.vector
        def _(dve):
            def body(job, b, j, n, g, first, before):
                if beside is not None and job is jobs[-1] and b in beside.vector:
                    beside.vector[b](dve)
                for s in range(CHUNKS):
                    if with_activations(before, s):
                        dve.wait_ge(act_high, s + 1)
                        part = slice(4 * s, 4 * s + 4)
                        dve.tensor_tensor(a_lo[:, part, :], a_raw[:, part, :], plain(a_hi[:, part, :]), ALU.subtract) \
                           .then_inc(act_low, 1)
                    if s == CHUNKS - 1 and before is not None and adds:
                        take_out(dve, *before)
                    dve.wait_ge(k.weights_high, n * CHUNKS + (s + 1))
                    raw = k.slots[:, s, 0:4 * job.cols]
                    dve.tensor_tensor(low(s, job), raw, plain(high(s, job)), ALU.subtract).then_inc(k.weights_low, 1)

            last = over_blocks(dve, body)
            if adds:
                take_out(dve, *last)
            if beside is not None:
                beside.vector[jobs[-1].blocks](dve)

        @block.tensor
        def _(pe):
            def body(job, b, j, n, g, first, before):
                banks = max(job.groups * job.unroll, 4)
                if j == 0 and first:
                    if jobs[0] is not job or k.evac0:
                        pe.wait_ge(k.group_out, evacs[jobs.index(job)])
                elif job.unroll == 2 and not first:
                    pe.wait_ge(k.group_out, g + (job.groups - 2 * job.groups))
                elif job.unroll == 1 and (b + 1) * job.groups > banks:
                    pe.wait_ge(k.group_out, g + job.groups - banks)
                for s in range(CHUNKS):
                    if with_activations(before, s):
                        pe.wait_ge(act_low, s + 1)
                    pe.wait_ge(k.weights_low, n * CHUNKS + (s + 1))
                    w_hi = shaped(high(s, job), 4, job.cols)
                    w_lo = shaped(low(s, job), 4, job.cols)
                    fold = job.kind == "fold"
                    for q in range(4):
                        kc = q if fold else 4 * s + q
                        kc_first, kc_last = (q == 0, q == 3) if fold else (kc == 0, kc == KC - 1)
                        for gi in range(NT if fold else job.groups):
                            group = s * NT + gi if fold else gi
                            at = ((b * job.groups if job.unroll == 1 else j * job.groups) + group) % (banks if job.unroll == 1 else 8)
                            bank = k.banks[at]
                            for part, (a, w) in enumerate(((a_hi, w_hi), (a_hi, w_lo), (a_lo, w_hi))):
                                start, stop = kc_first and part == 0, kc_last and part == 2
                                if job.kind == "feat":
                                    m = pe.matmul(bank[0:job.m, 0:T], w[:, q, gi * job.m:(gi + 1) * job.m], a[:, kc, :],
                                                  start=start, stop=stop)
                                else:
                                    m = pe.matmul(bank[:, 0:job.cols], a[:, kc, gi * P:(gi + 1) * P], w[:, q, :],
                                                  start=start, stop=stop)
                            if kc_last:
                                m.then_inc(k.group_done, 1)
                            elif q == 3 and gi == job.groups - 1:
                                m.then_inc(k.slot_used, 1)

            over_blocks(pe, body)

    k.block0, k.evac0 = after_blocks, after_groups


def normalise(k, name, src3, gain, dst3, load=None, upcoming=None, beside=None):
    nc = k.nc
    xs = shaped(k.mix_t[:, :], NT, D)
    area = Area(k.work[:, :])
    ms, sd, rstd = area.take(NT), area.take(NT), area.take(NT)
    squared, meaned, rooted = k.sem(name + "_squared"), k.sem(name + "_meaned"), k.sem(name + "_rooted")
    inverted, scaled, turned = k.sem(name + "_inverted"), k.sem(name + "_scaled"), k.sem(name + "_turned")
    own_squared, scaled_act = k.sem(name + "_own_squared"), k.sem(name + "_scaled_act")
    out_act, out_dve, arrived = k.sem(name + "_out_act"), k.sem(name + "_out_dve"), k.sem(name + "_arrived")

    with nc.Block() as block:
        @block.sync
        def _(sp):
            if load is not None:
                load(sp, arrived)
            if beside is not None:
                beside(sp)
            if upcoming is not None:
                start_stream(sp, k, upcoming)

        @block.scalar
        def _(act):
            if load is not None:
                act.wait_ge(arrived, 32)
            act.activation(xs[:, 0, :], src3[:, 0, :], ACT.Square, accum_out=ms[:, 0:1]).then_inc(squared, 1)
            act.wait_ge(meaned, 1)
            act.activation(sd[:, :], rstd[:, :], ACT.Sqrt).then_inc(rooted, 1)
            act.wait_ge(inverted, 1)
            act.activation(xs[:, 0, :], src3[:, 0, :], ACT.Copy, scale=ms[:, 0:1]).then_inc(scaled_act, 1)
            for kc in range(0, KC, 2):
                act.wait_ge(turned, kc + 1)
                act.activation(dst3[:, kc, :], k.banks[kc % 8][:, 0:T], ACT.Copy, scale=gain[:, kc:kc + 1]) \
                   .then_inc(out_act, 1)

        @block.vector
        def _(dve):
            if load is not None:
                dve.wait_ge(arrived, 32)
            dve.tensor_tensor_reduce(xs[:, 1, :], src3[:, 1, :], src3[:, 1, :], 1.0, 0.0, ALU.mult, ALU.add, ms[:, 1:2]) \
               .then_inc(own_squared, 1)
            dve.wait_ge(own_squared, 1)
            dve.wait_ge(squared, 1)
            dve.tensor_scalar(rstd[:, :], ms[:, :], 1.0 / D, EPS, ALU.mult, ALU.add).then_inc(meaned, 1)
            dve.wait_ge(rooted, 1)
            dve.reciprocal(ms[:, :], sd[:, :]).then_inc(inverted, 1)
            dve.wait_ge(inverted, 1)
            dve.tensor_scalar(xs[:, 1, :], src3[:, 1, :], ms[:, 1:2], None, ALU.mult).then_inc(scaled, 1)
            for kc in range(1, KC, 2):
                dve.wait_ge(turned, kc + 1)
                dve.tensor_scalar(dst3[:, kc, :], k.banks[kc % 8][:, 0:T], gain[:, kc:kc + 1], None, ALU.mult) \
                   .then_inc(out_dve, 1)

        @block.tensor
        def _(pe):
            if load is not None:
                pe.wait_ge(arrived, 32)
            pe.wait_ge(scaled_act, 1)
            pe.wait_ge(scaled, 1)
            for kc in range(KC):
                if kc >= 8:
                    pe.wait_ge(out_dve if kc % 2 else out_act, (kc - 8) // 2 + 1)
                for t in range(NT):
                    ins = pe.transpose(k.banks[kc % 8][:, t * P:(t + 1) * P], xs[:, t, kc * P:(kc + 1) * P],
                                       k.c("ident"))
                ins.then_inc(turned, 1)



def gla(k, name="gla", upcoming=None):
    nc, ins = k.nc, k.ins
    h3 = shaped(k.h[:, 0:NT * H_W], NT, H_W)
    gd = shaped(k.h[:, NT * H_W:NT * H_W + NT * 32], NT, 32)
    area = Area(k.act_t[:, :], k.work[:, :], k.mix_t[:, 4 * T:])
    up = area.take(512, parts=32)
    bias, out_g = area.take(512), area.take(512)
    gd_t = area.take(T, parts=32)
    la = area.take(NT, 512)
    tmp = area.take(NT, 512)
    grow = area.take(NT, 512)
    keep = area.take(2, NT, GLA_H, P)
    q_t = area.take(2, 2, T)
    k_t = area.take(2, 2, T)
    k_end = area.take(NT, 512)
    state = area.take(2, 2, 3, P)
    decay = area.take(2, 2, NT, 2)
    stats = area.take(3, NT * GLA_H)
    q_in, k_in = grow, la
    S = lambda n: k.sem(f"{name}_{n}")
    arrived, cleared = S("arrived"), S("cleared")
    dve_step, act_step = S("dve_step"), S("act_step")
    gates_turned, gates_out, logits, sized, exped, logged = (S(n) for n in (
        "gates_turned", "gates_out", "logits", "sized", "exped", "logged"))
    la_ready, sums, tails, exp_done, dec_done, q_done, k_done, ke_done = (S(n) for n in (
        "la_ready", "sums", "tails", "exp_done", "dec_done", "q_done", "k_done", "ke_done"))
    q_turned, q_out, k_turned, k_out, scores, kept, incs, states, o_done, o_sq, o_ms, o_sd, y_done, silu_done, y_turned, y_out = (
        S(n) for n in ("q_turned", "q_out", "k_turned", "k_out", "scores", "kept", "incs", "states", "o_done",
                       "o_sq", "o_ms", "o_sd", "y_done", "silu_done", "y_turned", "y_out"))
    B = k.banks
    y = tmp

    def o_at(t, hh):
        return B[1 + hh % 2][:, (t * 2 + hh // 2) * P:(t * 2 + hh // 2 + 1) * P]

    def inc_at(d, r, s):
        odd = (s if d == 0 else 3 - s) % 2
        n = (d * 2 + r) * 3 + s
        i = sum(1 for m in range(n) if ((m % 3) if m < 6 else 3 - m % 3) % 2 == odd)
        return ((5, 6), (7, 0))[odd][i // 4], i % 4 * P

    with nc.Block() as block:
        @block.sync
        def _(sp):
            sp.dma_start(up, ins["gla_up"]).then_inc(arrived, 16)
            sp.dma_start(bias, ins["gla_rows"][:, 0:512]).then_inc(arrived, 16)
            sp.dma_start(out_g, ins["gla_rows"][:, 512:1024]).then_inc(arrived, 16)
            if upcoming is not None:
                start_stream(sp, k, upcoming)

        @block.gpsimd
        def _(pool):
            pool.memset(keep[:, :, :, :], 0.0).then_inc(cleared, 1)

        @block.tensor
        def _(pe):
            for t in range(NT):
                m = pe.transpose(B[0][0:32, t * P:(t + 1) * P], gd[:, t, :], k.c("ident"))
            m.then_inc(gates_turned, 1)
            pe.wait_ge(gates_out, 1)
            pe.wait_ge(arrived, 48)
            for t in range(NT):
                pe.matmul(B[1 + t][:, :], gd_t[:, t * P:(t + 1) * P], up, start=True, stop=True).then_inc(logits, 1)
            pe.wait_ge(la_ready, 1)
            for t in range(NT):
                pe.matmul(B[1 + t][:, 0:256], k.c("tri_f"), la[:, t, 0:256], start=True, stop=True)
                pe.matmul(B[1 + t][:, 256:512], k.c("tri_b"), la[:, t, 256:512], start=True, stop=True).then_inc(sums, 1)
            for t in range(NT):
                pe.matmul(B[3 + t][:, :], k.c("same"), la[:, t, :], start=True, stop=True).then_inc(tails, 1)
            for d in range(2):
                for r in range(2):
                    for t in range(NT):
                        m = pe.matmul(B[5][:, (d * 2 + r) * 4 + 2 * t:(d * 2 + r) * 4 + 2 * t + 2],
                                      la[:, t, d * 256 + r * P:d * 256 + (r + 1) * P], k.c("half"), start=True, stop=True)
            m.then_inc(tails, 1)
            pe.wait_ge(ke_done, 2)
            for d in range(2):
                for r in range(2):
                    for s in range(3):
                        c = s if d == 0 else 3 - s
                        for e in range(2):
                            hh = 2 * r + e
                            rows = slice(64 * (c % 2), 64 * (c % 2) + 64)
                            bank, col = inc_at(d, r, s)
                            m = pe.matmul(B[bank][64 * e:64 * e + 64, col:col + P],
                                          k_end[rows, c // 2, d * 256 + hh * 64:d * 256 + hh * 64 + 64],
                                          h3[rows, c // 2, H_VA + hh * P:H_VA + (hh + 1) * P], start=True, stop=True)
            m.then_inc(incs, 1)
            for src, done, turned, out in ((q_in, q_done, q_turned, q_out), (k_in, k_done, k_turned, k_out)):
                pe.wait_ge(done, 2)
                for d in range(2):
                    if src is k_in:
                        pe.wait_ge(q_out, d + 1)
                    for r in range(2):
                        for t in range(NT):
                            m = pe.transpose(B[3 + d][:, r * T + t * P:r * T + (t + 1) * P],
                                             src[:, t, d * 256 + r * P:d * 256 + (r + 1) * P], k.c("ident"))
                    m.then_inc(turned, 1)
            pe.wait_ge(k_out, 2)
            for d in range(2):
                for e in range(2):
                    rows = slice(64 * e, 64 * e + 64)
                    for t in range(NT):
                        for r in range(2):
                            m = pe.matmul(B[1 + 2 * d + e][:, (t * 2 + r) * P:(t * 2 + r + 1) * P],
                                          k_t[rows, d, r, t * P:(t + 1) * P], q_t[rows, d, r, t * P:(t + 1) * P],
                                          start=True, stop=True)
                    m.then_inc(scores, 1)
            pe.wait_ge(kept, 4)
            pe.wait_ge(states, 1)
            for e in range(2):
                rows = slice(64 * e, 64 * e + 64)
                for t in range(NT):
                    for r in range(2):
                        hh = 2 * r + e
                        for d in range(2):
                            pe.matmul(o_at(t, hh), keep[:, d, e, 2 * t + r, :], h3[:, t, H_VA + hh * P:H_VA + (hh + 1) * P],
                                      start=d == 0, stop=False, skip_group_check=True)
                        for c in (2 * t, 2 * t + 1):
                            for d in range(2):
                                s = (c if d == 0 else 3 - c) - 1
                                if s >= 0:
                                    m = pe.matmul(o_at(t, hh)[64 * (c % 2):64 * (c % 2) + 64, :],
                                                  q_t[rows, d, r, c * 64:c * 64 + 64], state[rows, d, r, s, :],
                                                  start=False, stop=True, skip_group_check=True)
                m.then_inc(o_done, 1)
            for t in range(NT):
                pe.wait_ge(y_done, t + 1)
                for hh in range(GLA_H):
                    m = pe.transpose(B[3 + t][:, hh * P:(hh + 1) * P], y[:, t, hh * P:(hh + 1) * P], k.c("ident"))
                m.then_inc(y_turned, 1)

        @block.scalar
        def _(act):
            act.wait_ge(gates_turned, 1)
            act.activation(gd_t, B[0][0:32, 0:T], ACT.Copy).then_inc(gates_out, 1)
            act.wait_ge(sized, 1)
            act.activation(grow[:, :, :], tmp[:, :, :], ACT.Exp, scale=-1.0).then_inc(exped, 1)
            act.wait_ge(exped, 1)
            act.activation(tmp[:, :, :], grow[:, :, :], ACT.Ln, bias=1.0).then_inc(logged, 1)
            act.wait_ge(sums, 2)
            act.wait_ge(la_ready, 1)
            for t in range(NT):
                act.activation(grow[:, t, :], B[1 + t][:, :], ACT.Exp).then_inc(exp_done, 1)
            act.wait_ge(tails, 3)
            for t in range(NT):
                act.activation(la[:, t, :], B[1 + t][:, :], ACT.Exp, scale=-1.0).then_inc(exp_done, 1)
            act.activation(shaped(decay.rearrange("p a b c d -> p (a b c d)"), 16), B[5][:, 0:16], ACT.Exp).then_inc(dec_done, 1)
            act.wait_ge(dve_step, 1)
            for t in range(NT):
                act.activation(tmp[:, t, :], k_end[:, t, :], ACT.Exp).then_inc(exp_done, 1)
            for d in range(2):
                act.wait_ge(q_turned, d + 1)
                act.activation(q_t[:, d, :, :].rearrange("p a b -> p (a b)"), B[3 + d][:, :], ACT.Copy).then_inc(q_out, 1)
            for d in range(2):
                act.wait_ge(k_turned, d + 1)
                act.activation(k_t[:, d, :, :].rearrange("p a b -> p (a b)"), B[3 + d][:, :], ACT.Copy).then_inc(k_out, 1)
            act.wait_ge(ke_done, 2)
            act.activation(h3[:, :, H_RA:H_RA + 512], h3[:, :, H_RA:H_RA + 512], ACT.Silu).then_inc(silu_done, 1)
            for t in range(NT):
                act.wait_ge(o_done, 2)
                for hh in range(GLA_H):
                    act.activation(k_end[:, t, hh * P:(hh + 1) * P], o_at(t, hh), ACT.Square,
                                   accum_out=stats[:, 0, t * GLA_H + hh:t * GLA_H + hh + 1]).then_inc(o_sq, 1)
            act.wait_ge(o_ms, 1)
            act.activation(stats[:, 2, :], stats[:, 1, :], ACT.Sqrt).then_inc(o_sd, 1)
            for t in range(NT):
                act.wait_ge(y_turned, t + 1)
                act.activation(k.mix3[:, 0:4, t * P:(t + 1) * P], shaped(B[3 + t][:, :], 4, P), ACT.Copy).then_inc(y_out, 1)

        @block.vector
        def _(dve):
            step = Chain(dve, S("dve_own"))
            dve.wait_ge(arrived, 48)
            for t in range(NT):
                dve.wait_ge(logits, t + 1)
                step(dve.tensor_tensor(la[:, t, :], B[1 + t][:, :], bias, ALU.add))
            dve.scalar_tensor_tensor(tmp[:, :, :], la[:, :, :], -1.0, la[:, :, :], ALU.mult, ALU.max).then_inc(sized, 1)
            dve.wait_ge(logged, 1)
            dve.scalar_tensor_tensor(la[:, :, :], la[:, :, :], 0.0, tmp[:, :, :], ALU.min, ALU.subtract).then_inc(la_ready, 1)
            dve.wait_ge(tails, 2)
            dve.wait_ge(sums, 2)
            for t in range(NT):
                step(dve.tensor_copy(k_end[:, t, :], B[3 + t][:, :]))
            dve.wait_ge(exp_done, 4)
            for t in range(NT):
                m = dve.tensor_tensor(k_end[:, t, :], k_end[:, t, :], B[1 + t][:, :], ALU.subtract)
                if t:
                    m.then_inc(dve_step, 1)
            dve.wait_ge(exp_done, 6)
            for d in range(2):
                dve.tensor_tensor(k_end[:, :, d * 256:(d + 1) * 256], tmp[:, :, d * 256:(d + 1) * 256],
                                  h3[:, :, H_KA:H_KA + 256], ALU.mult).then_inc(ke_done, 1)
            for d in range(2):
                dve.scalar_tensor_tensor(q_in[:, :, d * 256:(d + 1) * 256], h3[:, :, H_QA:H_QA + 256], GLA_DK ** -0.5,
                                         grow[:, :, d * 256:(d + 1) * 256], ALU.mult, ALU.mult).then_inc(q_done, 1)
            for d in range(2):
                dve.tensor_tensor(k_in[:, :, d * 256:(d + 1) * 256], la[:, :, d * 256:(d + 1) * 256],
                                  h3[:, :, H_KA:H_KA + 256], ALU.mult).then_inc(k_done, 1)
            dve.wait_ge(incs, 1)
            dve.wait_ge(dec_done, 1)
            for s in range(3):
                for d in range(2):
                    for r in range(2):
                        bank, col = inc_at(d, r, s)
                        inc = B[bank][:, col:col + P]
                        if s == 0:
                            m = dve.tensor_copy(state[:, d, r, s, :], inc)
                        else:
                            c = s if d == 0 else 3 - s
                            m = dve.scalar_tensor_tensor(state[:, d, r, s, :], state[:, d, r, s - 1, :],
                                                         decay[:, d, r, c // 2, c % 2:c % 2 + 1], inc, ALU.mult, ALU.add)
                if s < 2:
                    step(m)
                else:
                    m.then_inc(states, 1)
            dve.wait_ge(cleared, 1)
            for d in range(2):
                for e in range(2):
                    dve.wait_ge(scores, 2 * d + e + 1)
                    dve.copy_predicated(keep[:, d, e, :, :].rearrange("p a b -> p (a b)"),
                                        k.c("keep_f" if d == 0 else "keep_b").bitcast(I32), B[1 + 2 * d + e][:, :]) \
                       .then_inc(kept, 1)
            dve.wait_ge(o_sq, NT * GLA_H)
            dve.tensor_scalar(stats[:, 1, :], stats[:, 0, :], 1.0 / GLA_DV, EPS, ALU.mult, ALU.add).then_inc(o_ms, 1)
            dve.wait_ge(o_sd, 1)
            step(dve.reciprocal(stats[:, 0, :], stats[:, 2, :]))
            dve.wait_ge(silu_done, 1)
            for t in range(NT):
                for hh in range(GLA_H):
                    i = t * GLA_H + hh
                    m = dve.tensor_scalar(y[:, t, hh * P:(hh + 1) * P], o_at(t, hh),
                                          stats[:, 0, i:i + 1], None, ALU.mult)
                step(m)
                step(dve.tensor_tensor(y[:, t, :], y[:, t, :], out_g, ALU.mult))
                dve.tensor_tensor(y[:, t, :], y[:, t, :], h3[:, t, H_RA:H_RA + 512], ALU.mult).then_inc(y_done, 1)



def attend(k, name, heads, q_t, k_t, v, bias, scale, out_t, area, gate=None, load=None, loads=0, upcoming=None):
    nc, B = k.nc, k.banks
    s_sb = area.take(2, NT, T)
    p_sb = area.take(2, NT, T)
    pt_sb = area.take(2, NT, T)
    top = area.take(heads, NT)
    den = area.take(2, heads, NT)
    S = lambda n: k.sem(f"{name}_{n}")
    scored, biased, topped, exped, divided, turned, taken, mixed, stored, arrived, inverted = (S(n) for n in (
        "scored", "biased", "topped", "exped", "divided", "turned", "taken", "mixed", "stored", "arrived", "inverted"))

    with nc.Block() as block:
        @block.sync
        def _(sp):
            if load is not None:
                load(sp, arrived)
            if upcoming is not None:
                start_stream(sp, k, upcoming)

        @block.tensor
        def _(pe):
            for i in range(heads + 3):
                if i < heads:
                    if i >= 2:
                        pe.wait_ge(biased, i - 1)
                    for t in range(NT):
                        m = pe.matmul(B[i % 2][:, t * T:(t + 1) * T], q_t(i)[:, t * P:(t + 1) * P], k_t(i), start=True, stop=True)
                    m.then_inc(scored, 1)
                if 2 <= i <= heads + 1:
                    h = i - 2
                    pe.wait_ge(divided, 2 * h + 2)
                    if h >= 2:
                        pe.wait_ge(taken, h - 1)
                    for t in range(NT):
                        for s in range(NT):
                            m = pe.transpose(B[2 + h % 2][:, s * T + t * P:s * T + (t + 1) * P],
                                             p_sb[:, h % 2, t, s * P:(s + 1) * P], k.c("ident"))
                    m.then_inc(turned, 1)
                if i >= 3:
                    h = i - 3
                    pe.wait_ge(taken, h + 1)
                    if h >= 2:
                        pe.wait_ge(stored, h - 1)
                    for s in range(NT):
                        m = pe.matmul(B[4 + h % 2][:, 0:T], v(h, s), pt_sb[:, h % 2, s, :], start=s == 0, stop=s == NT - 1)
                    m.then_inc(mixed, 1)

        @block.vector
        def _(dve):
            if load is not None:
                dve.wait_ge(arrived, 16 * loads)
            for i in range(heads + 3):
                if i < heads:
                    dve.wait_ge(scored, i + 1)
                    if i >= 2:
                        dve.wait_ge(exped, 2 * (i - 1))
                    flat = s_sb[:, i % 2, :, :].rearrange("p a b -> p (a b)")
                    if bias is None:
                        dve.tensor_scalar(flat, B[i % 2][:, :], scale, None, ALU.mult).then_inc(biased, 1)
                    else:
                        dve.scalar_tensor_tensor(flat, B[i % 2][:, :], scale, bias(i).rearrange("p a b -> p (a b)"),
                                                 ALU.mult, ALU.add).then_inc(biased, 1)
                    dve.wait_ge(biased, i + 1)
                    dve.tensor_reduce(top[:, i, :], s_sb[:, i % 2, :, :], AX.X, ALU.max, negate=True).then_inc(topped, 1)
                if 1 <= i <= heads:
                    h = i - 1
                    dve.wait_ge(exped, 2 * h + 2)
                    dve.reciprocal(den[:, 1, h, :], den[:, 0, h, :]).then_inc(inverted, 1)
                    dve.wait_ge(inverted, h + 1)
                    for t in range(NT):
                        dve.tensor_scalar(p_sb[:, h % 2, t, :], p_sb[:, h % 2, t, :], den[:, 1, h, t:t + 1], None,
                                          ALU.mult).then_inc(divided, 1)
                if i >= 3:
                    h = i - 3
                    dve.wait_ge(mixed, h + 1)
                    if gate is None:
                        dve.tensor_copy(out_t(h), B[4 + h % 2][:, 0:T]).then_inc(stored, 1)
                    else:
                        dve.tensor_tensor(out_t(h), B[4 + h % 2][:, 0:T], gate(h), ALU.mult).then_inc(stored, 1)

        @block.scalar
        def _(act):
            for i in range(heads + 2):
                if i < heads:
                    act.wait_ge(topped, i + 1)
                    if i >= 2:
                        act.wait_ge(turned, i - 1)
                    for t in range(NT):
                        act.activation(p_sb[:, i % 2, t, :], s_sb[:, i % 2, t, :], ACT.Exp, bias=top[:, i, t:t + 1],
                                       accum_out=den[:, 0, i, t:t + 1]).then_inc(exped, 1)
                if i >= 2:
                    h = i - 2
                    act.wait_ge(turned, h + 1)
                    if h >= 2:
                        act.wait_ge(mixed, h - 1)
                    act.activation(pt_sb[:, h % 2, :, :].rearrange("p a b -> p (a b)"), B[2 + h % 2][:, :], ACT.Copy) \
                       .then_inc(taken, 1)


def dilated_rotate(k, groups_before, name="dil"):
    h3 = shaped(k.h[:, 0:NT * H_W], NT, H_W)
    NH = 2 * DIL_H
    area = Area(k.work[:, :])
    gains = area.take(2, HD)
    ss = area.take(NT, NH)
    sd = area.take(NT, NH)
    rs = area.take(NT, NH)
    sq = area.take(NH, HD)
    rot = shaped(sq.rearrange("p a b -> p (a b)")[:, 0:4 * NH * HALF], 4, NH, HALF)
    arrived, meaned, rooted, own = (k.sem(f"{name}_{n}") for n in ("arrived", "meaned", "rooted", "own"))
    qk = [h3[:, t, H_QD:H_QD + NH * HD].rearrange("p (h e) -> p h e", h=NH) for t in range(NT)]
    cos, sin = k.c("cos", NT, HALF), k.c("sin", NT, HALF)
    count = [0]

    def step(dve, m):
        count[0] += 1
        m.then_inc(own, 1)
        dve.wait_ge(own, count[0])

    def sums(dve, t):
        if t == 0:
            dve.wait_ge(k.group_out, groups_before)
        step(dve, dve.tensor_tensor(sq[:, :, :], qk[t], qk[t], ALU.mult))
        step(dve, dve.tensor_reduce(ss[:, t, :], sq[:, :, :], AX.X, ALU.add))
        if t == NT - 1:
            dve.tensor_scalar(ss[:, :, :], ss[:, :, :], 1.0 / HD, EPS, ALU.mult, ALU.add).then_inc(meaned, 1)

    def root(act):
        act.wait_ge(meaned, 1)
        act.activation(sd[:, :, :], ss[:, :, :], ACT.Sqrt).then_inc(rooted, 1)

    def rotate(dve, half, t):
        if half == t == 0:
            dve.wait_ge(rooted, 1)
            step(dve, dve.reciprocal(rs[:, :, :], sd[:, :, :]))
            dve.wait_ge(arrived, 16)
        hs = slice(half * DIL_H, (half + 1) * DIL_H)
        a = qk[t][:, hs, :]
        wide = lambda ap, n: ap.unsqueeze(2).to_broadcast([P, DIL_H, n])
        step(dve, dve.tensor_tensor(a, a, wide(rs[:, t, hs], HD), ALU.mult))
        step(dve, dve.tensor_tensor(a, a, gains[:, half, :].unsqueeze(1).to_broadcast([P, DIL_H, HD]), ALU.mult))
        x1, x2 = a[:, :, 0:HALF], a[:, :, HALF:ROPE]
        over = lambda ap: ap.unsqueeze(1).to_broadcast([P, DIL_H, HALF])
        c, s = over(cos[:, t, :]), over(sin[:, t, :])
        dve.tensor_tensor(rot[:, 0, hs, :], x1, c, ALU.mult)
        dve.tensor_tensor(rot[:, 1, hs, :], x2, s, ALU.mult)
        dve.tensor_tensor(rot[:, 2, hs, :], x2, c, ALU.mult)
        step(dve, dve.tensor_tensor(rot[:, 3, hs, :], x1, s, ALU.mult))
        dve.tensor_tensor(x1, rot[:, 0, hs, :], rot[:, 1, hs, :], ALU.subtract)
        step(dve, dve.tensor_tensor(x2, rot[:, 2, hs, :], rot[:, 3, hs, :], ALU.add))

    return Beside(
        lambda sp: sp.dma_start(gains, shaped(k.ins["qk_gain"], 2, HD)).then_inc(arrived, 16),
        {1: lambda dve: sums(dve, 0), 2: lambda dve: sums(dve, 1), 3: lambda dve: rotate(dve, 0, 0),
         4: lambda dve: rotate(dve, 0, 1), 5: lambda dve: rotate(dve, 1, 0), 6: lambda dve: rotate(dve, 1, 1)},
        {3: root})


def dilated_turn(k, name="dil_turn", upcoming=None):
    nc, B = k.nc, k.banks
    h3 = shaped(k.h[:, 0:NT * H_W], NT, H_W)
    NH = 2 * DIL_H
    turned_t = k.work[:, 0:NH * T]
    turned, taken_a, taken_d = (k.sem(f"{name}_{n}") for n in ("turned", "taken_a", "taken_d"))
    qk = [h3[:, t, H_QD:H_QD + NH * HD].rearrange("p (h e) -> p h e", h=NH) for t in range(NT)]
    BT = 4

    def dst(n):
        return turned_t[:, n * 2 * T:(n + 1) * 2 * T]

    with nc.Block() as block:
        @block.sync
        def _(sp):
            if upcoming is not None:
                start_stream(sp, k, upcoming)

        @block.scalar
        def _(act):
            for n in range(0, NT * NH // BT, 2):
                act.wait_ge(turned, n + 1)
                act.activation(dst(n), B[n % 8][:, :], ACT.Copy).then_inc(taken_a, 1)

        @block.tensor
        def _(pe):
            for n in range(NT * NH // BT):
                if n >= 8:
                    pe.wait_ge(taken_d if n % 2 else taken_a, (n - 8) // 2 + 1)
                for e in range(2):
                    for t in range(NT):
                        m = pe.transpose(B[n % 8][:, e * T + t * P:e * T + (t + 1) * P], qk[t][:, 2 * n + e, :], k.c("ident"))
                m.then_inc(turned, 1)

        @block.vector
        def _(dve):
            for n in range(1, NT * NH // BT, 2):
                dve.wait_ge(turned, n + 1)
                dve.tensor_copy(dst(n), B[n % 8][:, :]).then_inc(taken_d, 1)





def load_query(sp, k, head, loaded):
    w = k.ins["w_query"][head] if head < PEER_H else k.ins["xa_wkv"][head - PEER_H]
    sp.dma_start(shaped(k.h[:, (head % 2) * 4096:(head % 2 + 1) * 4096], KC, 2 * PEER_K), w) \
      .then_inc(loaded[head % 2], 16)


def peer(k, query_in, name="peer"):
    nc, ins, B = k.nc, k.ins, k.banks
    UNITS, K = NT * PEER_H, PEER_TOP
    DEPTH = NSLOT // 2
    wq = shaped(k.h[:, 0:8192], 2, KC, 2 * PEER_K)
    keys = shaped(k.h[:, 8192:10240], 2 * PEER_H, PEER_K)
    gain = k.h[:, 10240:12288]
    q_t = shaped(k.h[:, 12288:13312], 2, 2, T)
    xn = shaped(k.mix_t[:, :], NT, D)
    mem = shaped(k.h[:, 8192:12288], NT, D)
    mem_k = k.mem_kv[:, 0:XA_H * T]
    mem_v = shaped(k.mem_kv[:, XA_H * T:], NT, XA_H * HD)
    LAST = PEER_H + 4
    area = Area(k.work[:, :])
    mem_ms, mem_sd, mem_rstd = area.take(NT), area.take(NT), area.take(NT)
    staged = area.take(2, 2, PEER_K)
    later = area.take(PEER_H, 2 * PEER_K)
    rest = area.take(2, PEER_K)
    cand = area.take(2, K, K)
    hot = area.take(2, K, K)
    top = area.take(2, 2, K)
    top_i = area.take(2, K).bitcast(U32)
    top_f = area.take(2, K)
    best = area.take(2, K)
    best_i = area.take(K).bitcast(U32)
    part_i = area.take(2, K).bitcast(U32)
    part_f = area.take(2, K)
    pair = area.take(2, K)
    rows_d = area.take(2, K).bitcast(U32)
    rows_u = area.take(2, K).bitcast(U32)
    e_best = area.take(2, K)
    low = area.take(2, 1)
    total = area.take(2, 1)
    inv = area.take(2, 1)
    dots = area.take(2, K)
    gelu = area.take(2, K)
    coef = area.take(2, K)
    diag = area.take(DEPTH, P)
    S = lambda n: k.sem(f"{name}_{n}")
    query_done, query_out, gain_in = S("query_done"), S("query_out"), S("gain_in")
    arrived, scored, stored, staged_done, selected, gated, gelu_done, coef_done, rows_u_ready = (S(n) for n in (
        "arrived", "scored", "stored", "staged", "selected", "gated", "gelu_done", "coef_done", "rows_u_ready"))
    down_used, up_used, diag_ready, acc_out, own = (S(n) for n in ("down_used", "up_used", "diag_ready", "acc_out", "own"))
    mem_in, mem_squared, mem_meaned, mem_rooted, mem_own, mem_scaled, mem_turned, mem_out = (S(n) for n in (
        "mem_in", "mem_squared", "mem_meaned", "mem_rooted", "mem_own", "mem_scaled", "mem_turned", "mem_out"))
    TURNS = KC // 2
    down_in = [S(f"down_in{i}") for i in range(DEPTH)]
    up_in = [S(f"up_in{i}") for i in range(DEPTH)]
    down_row = lambda j: k.slots[:, j % DEPTH, :]
    up_row = lambda j: k.slots[:, DEPTH + j % DEPTH, :]

    def walk(unit):
        def over(eng):
            for t in range(NT):
                n0 = t * PEER_H
                unit(n0, 0, t)
                unit(n0 + 1, 1, t)
                with eng.Fori(1, PEER_H // 2 - 1) as i:
                    for p in range(2):
                        unit(2 * i + (n0 + p), p, t, inner=True)
                unit(n0 + PEER_H - 2, 0, t)
                unit(n0 + PEER_H - 1, 1, t)
            unit(UNITS, 0, NT)
        return over

    with nc.Block() as block:
        @block.sync
        def _(sp):
            sp.dma_start(keys, ins["sub_keys"]).then_inc(arrived, 16)
            sp.dma_start(gain, ins["norm2_row"]).then_inc(gain_in, 16)
            for head in range(2, PEER_H):
                sp.wait_ge(query_done, head - 1)
                load_query(sp, k, head, query_in)
            sp.wait_ge(scored, PEER_H)
            sp.dma_start(mem, ins["mem"].rearrange("(t p) d -> p t d", p=P)).then_inc(mem_in, 16)
            for head in range(PEER_H, LAST):
                sp.wait_ge(query_done, head - 1)
                load_query(sp, k, head, query_in)

        @block.tensor
        def _(pe):
            def query(head, p, part=None, of_memory=False):
                bank = B[4 + p]
                if part is None or part == 0:
                    pe.wait_ge(query_in[p], head * 8 + (16 - 8 * p))
                    if of_memory:
                        pe.wait_ge(query_out, head - 1)
                        pe.wait_ge(mem_out, TURNS)
                for i in range(2 * KC) if part is None else (2 * part, 2 * part + 1):
                    f, kc = divmod(i, KC)
                    if of_memory and p == 1:
                        a, w = k.act3[:, kc, f * P:(f + 1) * P], wq[:, p, kc, :]
                    else:
                        a, w = wq[:, p, kc, f * PEER_K:(f + 1) * PEER_K], k.act3[:, kc, :]
                    m = pe.matmul(bank[:, f * T:(f + 1) * T], a, w, start=kc == 0, stop=kc == KC - 1)
                if i == 2 * KC - 1:
                    m.then_inc(query_done, 1)

            def score(head, p, before):
                pe.wait_ge(query_out, head + 1)
                if before:
                    pe.wait_ge(stored, head - 1)
                for t in range(NT):
                    for c in range(2):
                        key = keys[:, 2 * head + c, :] if isinstance(head, int) else \
                            keys[:, bass.ds(2 * head + c, 1), :].rearrange("p a b -> p (a b)")
                        m = pe.matmul(B[6 + p][:, (t * 2 + c) * PEER_K:(t * 2 + c + 1) * PEER_K],
                                      q_t[:, p, c, t * P:(t + 1) * P], key, start=True, stop=True)
                m.then_inc(scored, 1)

            for head in range(2):
                query(head, head)
                if head == 0:
                    pe.wait_ge(arrived, 16)
                score(head, head, False)

            def unit(n, p, t, inner=False):
                ahead = t == 0 and (inner or n < PEER_H - 2)
                if not inner and n == 0:
                    query(2, 0)
                    score(2, 0, True)
                    return
                for j in range(K):
                    first = not inner and n % PEER_H == 1 and j == 0
                    last = not inner and n % PEER_H == 0 and j == K - 1
                    if first and n > 1:
                        pe.wait_ge(acc_out, 4)
                    if ahead:
                        query(n + 2, p, part=j)
                    if t == 1 and inner:
                        query(n - 2, p, part=j, of_memory=True)
                    if not inner and n == PEER_H + 1 and j % 2 == 0:
                        g = j // 2
                        if g == 0:
                            pe.wait_ge(mem_scaled, NT)
                            pe.wait_ge(stored, PEER_H)
                        if g >= 4:
                            pe.wait_ge(mem_out, g - 3)
                        for e in range(2):
                            for tt in range(NT):
                                m = pe.transpose(B[4 + g % 4][:, e * T + tt * P:e * T + (tt + 1) * P],
                                                 mem[:, tt, (2 * g + e) * P:(2 * g + e + 1) * P], k.c("ident"))
                        m.then_inc(mem_turned, 1)
                    pe.wait_ge(diag_ready, n * K + (j + 1 - K))
                    pe.wait_ge(up_in[j % DEPTH], n * (16 * K // DEPTH) + 16 * (j // DEPTH + 1 - K // DEPTH))
                    for c in range(4):
                        m = pe.matmul(B[c][:, :], diag[:, j % DEPTH, :], up_row(j)[:, c * 512:(c + 1) * 512],
                                      start=first, stop=last)
                    m.then_inc(up_used, 1)
                if ahead:
                    score(n + 2, p, True)

            walk(unit)(pe)

        @block.scalar
        def _(act):
            flat = lambda a: a.rearrange("p a b -> p (a b)")

            act_rows = shaped(k.act_t[:, :], NT, D)

            def take_query(head, p):
                act.wait_ge(query_done, head + 1)
                act.activation(flat(q_t[:, p, :, :]), B[4 + p][:, :], ACT.Copy).then_inc(query_out, 1)

            def stage(n, p, direct):
                if not isinstance(n, int) or n >= 2:
                    act.wait_ge(selected, n - 1)
                if direct:
                    act.wait_ge(scored, n + 1)
                    act.activation(flat(staged[:, p, :, :]), B[6 + p][:, 0:256], ACT.Copy).then_inc(staged_done, 1)
                    keep = later[:, n, :] if isinstance(n, int) else flat(later[:, bass.ds(n, 1), :])
                    act.activation(keep, B[6 + p][:, 256:512], ACT.Copy).then_inc(stored, 1)
                    return
                if isinstance(n, int) and n == PEER_H:
                    act.wait_ge(stored, PEER_H)
                src = later[:, n - PEER_H, :] if isinstance(n, int) else flat(later[:, bass.ds(n - PEER_H, 1), :])
                act.activation(flat(staged[:, p, :, :]), src, ACT.Copy).then_inc(staged_done, 1)

            def gate(n, p):
                act.wait_ge(selected, n + 1)
                act.activation(e_best[:, p, :], best[:, p, :], ACT.Exp, bias=low[:, p, :], accum_out=total[:, p, :]) \
                   .then_inc(gated, 1)

            take_query(0, 0)
            stage(0, 0, True)
            take_query(1, 1)
            gate(0, 0)

            def unit(n, p, t, inner=False):
                more = inner or n < UNITS - 1
                if more:
                    stage(n + 1, 1 - p, t == 0 and (inner or n < PEER_H - 1))
                for j in range(K):
                    if j == K // 2 and more:
                        gate(n + 1, 1 - p)
                    if inner or n > 0:
                        if j == 0:
                            act.wait_ge(coef_done, n + 0)
                        if inner or n > 1 or j >= DEPTH:
                            act.wait_ge(up_used, n * K + (j + 1 - DEPTH - K))
                        act.activation(diag[:, j % DEPTH, :], k.c("ident"), ACT.Copy, scale=coef[:, 1 - p, j:j + 1]) \
                           .then_inc(diag_ready, 1)
                    if not inner and n == PEER_H - 1 and j == 4:
                        act.wait_ge(mem_in, 16)
                        for tt in range(NT):
                            act.activation(act_rows[:, tt, :], mem[:, tt, :], ACT.Square, accum_out=mem_ms[:, tt:tt + 1]) \
                               .then_inc(mem_squared, 1)
                    if not inner and n == PEER_H and j == 4:
                        act.wait_ge(mem_meaned, 1)
                        act.activation(mem_sd, mem_rstd, ACT.Sqrt).then_inc(mem_rooted, 1)
                    if not inner and n == PEER_H + 1 and j % 2 == 1:
                        g = j // 2
                        act.wait_ge(mem_turned, g + 1)
                        for e in range(2):
                            kc = 2 * g + e
                            m = act.activation(k.act3[:, kc, :], B[4 + g % 4][:, e * T:(e + 1) * T], ACT.Copy,
                                               scale=k.c("mem_g")[:, kc:kc + 1])
                        m.then_inc(mem_out, 1)
                if t == 0 and (inner or n < PEER_H - 2):
                    take_query(n + 2, p)
                if t == 1 and inner:
                    act.wait_ge(query_done, n - 1)
                    if p == 0:
                        dst, src = mem_k[:, bass.ds(n * 256 - (PEER_H + 2) * 256, 512)], B[4][:, :]
                    else:
                        dst, src = mem_v[:, :, bass.ds(n * P - (PEER_H + 3) * P, 256)], shaped(B[5][:, :], NT, 256)
                    act.activation(dst, src, ACT.Copy).then_inc(query_out, 1)
                if inner or n < UNITS:
                    act.wait_ge(down_used, n * K + K)
                    act.activation(gelu[:, p, :], dots[:, p, :], ACT.Gelu_apprx_tanh).then_inc(gelu_done, 1)

            walk(unit)(act)

        @block.gpsimd
        def _(pool):
            def unit(n, p, t, inner=False):
                for j in range(K):
                    if inner or n < UNITS:
                        if j == 0:
                            pool.wait_ge(selected, n + 1)
                        if inner or n > 0 or j >= DEPTH:
                            pool.wait_ge(down_used, n * K + (j + 1 - DEPTH))
                        pool.nop(nofuse=True)
                        pool.indirect_dma_start(down_row(j), None, ins["peer_down"],
                                                bass.IndirectOffsetOnAxis(ap=rows_d[:, p, j:j + 1], axis=0)) \
                            .then_inc(down_in[j % DEPTH], 16)
                    if inner or n > 0:
                        if j == 0:
                            pool.wait_ge(rows_u_ready, n + 0)
                        if inner or n > 1 or j >= DEPTH:
                            pool.wait_ge(up_used, n * K + (j + 1 - DEPTH - K))
                        pool.nop(nofuse=True)
                        pool.indirect_dma_start(up_row(j), None, ins["peer_up"],
                                                bass.IndirectOffsetOnAxis(ap=rows_u[:, 1 - p, j:j + 1], axis=0)) \
                            .then_inc(up_in[j % DEPTH], 16)

            walk(unit)(pool)

        @block.vector
        def _(dve):
            own_step = Chain(dve, own)

            def first_step(ins_):
                own_step(ins_)

            dve.wait_ge(gain_in, 16)
            for t in range(NT):
                first_step(dve.tensor_tensor(xn[:, t, :], xn[:, t, :], gain, ALU.mult))

            def select(n, p, count):
                done = [0]

                def step(m):
                    done[0] += 1
                    m.then_inc(own, 1)
                    dve.wait_ge(own, count + done[0])

                def top16(src, values, index, rest_):
                    dve.nop(nofuse=True)
                    step(dve.max(values[:, 0:8], src))
                    dve.nop(nofuse=True)
                    dve.max_index(index[:, 0:8], values[:, 0:8], src)
                    step(dve.match_replace(rest_, values[:, 0:8], src, -3.0e38))
                    dve.nop(nofuse=True)
                    step(dve.max(values[:, 8:16], rest_))
                    dve.nop(nofuse=True)
                    step(dve.max_index(index[:, 8:16], values[:, 8:16], rest_))

                dve.wait_ge(staged_done, n + 1)
                for c in range(2):
                    top16(staged[:, p, c, :], top[:, p, c, :], top_i[:, c, :], rest[:, c, :])
                dve.tensor_copy(top_f[:, :, :], top_i[:, :, :])
                step(dve.tensor_tensor(cand[:, 0, :, :], top[:, p, 0, :].unsqueeze(2).to_broadcast([P, K, K]),
                                       top[:, p, 1, :].unsqueeze(1).to_broadcast([P, K, K]), ALU.add))
                flat = lambda a: a.rearrange("p a b -> p (a b)")
                top16(flat(cand[:, 0, :, :]), best[:, p, :], best_i, flat(cand[:, 1, :, :]))
                dve.tensor_scalar(low[:, p, :], best[:, p, 0:1], -1.0, None, ALU.mult)
                dve.tensor_scalar(part_i[:, 0, :], best_i, 4, None, ALU.logical_shift_right)
                step(dve.tensor_scalar(part_i[:, 1, :], best_i, 15, None, ALU.bitwise_and))
                step(dve.tensor_copy(part_f[:, :, :], part_i[:, :, :]))
                for c in range(2):
                    m = dve.tensor_tensor(hot[:, c, :, :], part_f[:, c, :].unsqueeze(2).to_broadcast([P, K, K]),
                                          k.c("iota").unsqueeze(1).to_broadcast([P, K, K]), ALU.is_equal)
                step(m)
                for c in range(2):
                    m = dve.tensor_tensor(hot[:, c, :, :], hot[:, c, :, :], top_f[:, c, :].unsqueeze(1).to_broadcast([P, K, K]),
                                          ALU.mult)
                step(m)
                step(dve.tensor_reduce(pair[:, :, :], hot[:, :, :, :], AX.X, ALU.add))
                dve.scalar_tensor_tensor(rows_d[:, p, :], pair[:, 0, :], float(PEER_K), pair[:, 1, :], ALU.mult, ALU.add) \
                   .then_inc(selected, 1)
                return done[0]

            per_unit = select(0, 0, own_step.count)
            base = own_step.count + per_unit
            PER = per_unit + 1

            def unit(n, p, t, inner=False):
                if not inner and n % PEER_H == 1 and n > 1:
                    take_sums(0, 0)
                if not inner and n == UNITS:
                    take_sums(1, 4)
                    return
                for j in range(K):
                    if j == DEPTH and (inner or n < UNITS - 1):
                        select(n + 1, 1 - p, n * PER + base)
                    if not inner and n == PEER_H - 1 and j == 12:
                        dve.wait_ge(mem_squared, NT)
                        dve.tensor_scalar(mem_rstd, mem_ms, 1.0 / D, EPS, ALU.mult, ALU.add).then_inc(mem_meaned, 1)
                    if not inner and n == PEER_H and j == 12:
                        dve.wait_ge(mem_rooted, 1)
                        dve.reciprocal(mem_ms, mem_sd).then_inc(mem_own, 1)
                        dve.wait_ge(mem_own, 1)
                        for tt in range(NT):
                            dve.tensor_scalar(mem[:, tt, :], mem[:, tt, :], mem_ms[:, tt:tt + 1], None, ALU.mult) \
                               .then_inc(mem_scaled, 1)
                    if j == K // 2:
                        if inner or n > 1:
                            dve.wait_ge(up_used, n * K - K)
                        dve.tensor_copy(rows_u[:, p, :], rows_d[:, p, :]).then_inc(rows_u_ready, 1)
                    dve.wait_ge(down_in[j % DEPTH], n * (16 * K // DEPTH) + 16 * (j // DEPTH + 1))
                    dve.tensor_tensor_reduce(down_row(j), down_row(j), xn[:, t, :], 1.0, 0.0, ALU.mult, ALU.add,
                                             dots[:, p, j:j + 1]).then_inc(down_used, 1)
                dve.wait_ge(gated, n + 1)
                dve.reciprocal(inv[:, p, :], total[:, p, :]).then_inc(own, 1)
                dve.wait_ge(own, n * PER + (base + PER if inner or n < UNITS - 1 else base + 1))
                dve.wait_ge(gelu_done, n + 1)
                dve.scalar_tensor_tensor(coef[:, p, :], gelu[:, p, :], inv[:, p, :], e_best[:, p, :], ALU.mult, ALU.mult) \
                   .then_inc(coef_done, 1)

            def take_sums(t, before):
                dve.wait_ge(up_used, (t + 1) * PEER_H * K)
                for c in range(4):
                    dst = k.x3[:, t, c * 512:(c + 1) * 512]
                    dve.tensor_tensor(dst, B[c][:, :], dst, ALU.add).then_inc(acc_out, 1)

            walk(unit)(dve)



S_LRU_X, S_LRU_Z, S_ML_U, S_MO_Q, S_MO_K, S_MO_Z, S_TOK = 0, 1024, 2048, 4096, 5632, 7168, 8704
TOK_W = 2 * ML_W + MO_W
LOG1P_TERMS = 8


def conv(dve, step, out, x, w, b, chunks):
    for c in range(chunks):
        m = dve.tensor_scalar(out[:, c, :], x[:, c, :], w[:, c, TAPS - 1:TAPS], b[:, c:c + 1], ALU.mult, ALU.add)
    step(m)
    for back in range(1, TAPS):
        for c in range(chunks):
            m = dve.scalar_tensor_tensor(out[:, c, back:], x[:, c, 0:T - back], w[:, c, TAPS - 1 - back:TAPS - back],
                                         out[:, c, back:], ALU.mult, ALU.add)
        step(m)


class MlstmWeights:

    def __init__(self, k):
        self.k = k
        area = Area(k.work[:, 5648:6128])
        self.cols = area.take(MLC * (TAPS + 1), parts=ML_C)
        self.bias = area.take(8)
        self.blk_w = area.take(3, MLC, 4, parts=ML_C)
        self.rest = area
        self.bd = Area(k.mix_t[:, 4 * T:]).take(3, MLC, ML_C, parts=ML_C)
        self.arrived = k.sem("ml_weights_arrived")

    def load(self, sp):
        sp.dma_start(self.cols, self.k.ins["ml_cols"]).then_inc(self.arrived, 16)
        sp.dma_start(self.blk_w, self.k.ins["ml_qkv"]).then_inc(self.arrived, 16)
        sp.dma_start(self.bias, self.k.ins["ml_rows"][:, 0:8]).then_inc(self.arrived, 16)

    def build(self, dve):
        dve.wait_ge(self.arrived, 48)
        mask = self.k.c("group")[0:ML_C, :]
        for i in range(3):
            for c in range(MLC):
                dve.tensor_tensor(self.bd[:, i, c, :].rearrange("p (g o) -> p g o", o=4),
                                  self.blk_w[:, i, c, :].unsqueeze(1).to_broadcast([ML_C, ML_C // 4, 4]),
                                  mask.unsqueeze(2).to_broadcast([ML_C, ML_C // 4, 4]), ALU.mult)


def rg_lru(k, ml, name="lru"):
    nc, ins, B = k.nc, k.ins, k.banks
    CH = LRU_W // P
    x = shaped(k.h[:, S_LRU_X:S_LRU_X + CH * T], CH, T)
    z = shaped(k.h[:, S_LRU_Z:S_LRU_Z + CH * T], CH, T)
    area = Area(k.act_t[:, :], k.work[:, 0:6128])
    xc, r, gate_i, a, th = (area.take(CH, T) for _ in range(5))
    wa, wx = area.take(CH, P), area.take(CH, P)
    par = area.take(CH * (TAPS + 4))
    conv_w = shaped(par[:, 0:CH * TAPS], CH, TAPS)
    conv_b, ba, bx, lam = (par[:, CH * (TAPS + i):CH * (TAPS + i + 1)] for i in range(4))
    size, e, q, z1, z2, sp, decay, growth = (area.take(CH) for _ in range(8))
    S = lambda n: k.sem(f"{name}_{n}")
    arrived, own, e_asked, e_done, conv_done, gates_in, gates_out, dec_done, exps, uu, rooted, silued, done = (S(n) for n in (
        "arrived", "own", "e_asked", "e_done", "conv_done", "gates_in", "gates_out", "dec_done", "exps", "uu", "rooted",
        "silued", "done"))

    with nc.Block() as block:
        @block.sync
        def _(sp):
            sp.dma_start(par, ins["lru_cols"]).then_inc(arrived, 16)
            sp.dma_start(wa, ins["lru_wa"]).then_inc(arrived, 16)
            sp.dma_start(wx, ins["lru_wx"]).then_inc(arrived, 16)
            ml.load(sp)

        @block.vector
        def _(dve):
            step = Chain(dve, own)
            dve.wait_ge(arrived, 48)
            step(dve.scalar_tensor_tensor(size, lam, -1.0, lam, ALU.mult, ALU.max))
            step(dve.tensor_scalar(e, size, -1.0, None, ALU.mult))
            dve.tensor_scalar(sp, lam, -1.0, 0.0, ALU.mult, ALU.max).then_inc(e_asked, 1)
            conv(dve, step, xc, x, conv_w, conv_b, CH)
            dve.tensor_copy(q, sp).then_inc(conv_done, 1)
            dve.wait_ge(e_done, 1)
            step(dve.tensor_scalar(z1, size, 2.0, None, ALU.add))
            step(dve.reciprocal(z2, z1))
            step(dve.tensor_tensor(z1, size, z2, ALU.mult))
            step(dve.tensor_tensor(z2, z1, z1, ALU.mult))
            step(dve.tensor_scalar(q, z2, 1.0 / (2 * LOG1P_TERMS + 1), None, ALU.mult))
            for n in range(LOG1P_TERMS - 1, 0, -1):
                step(dve.scalar_tensor_tensor(q, q, 1.0 / (2 * n + 1), z2, ALU.add, ALU.mult))
            step(dve.scalar_tensor_tensor(q, q, 1.0, z1, ALU.add, ALU.mult))
            step(dve.scalar_tensor_tensor(sp, q, 2.0, sp, ALU.mult, ALU.add))
            dve.tensor_scalar(decay, sp, -8.0, None, ALU.mult)
            dve.tensor_scalar(growth, sp, 8.0, None, ALU.mult).then_inc(dec_done, 1)
            ml.build(dve)
            dve.wait_ge(exps, 2 * CH)
            step(dve.tensor_tensor(r, a, a, ALU.mult))
            dve.scalar_tensor_tensor(th, r, 1.0, th, ALU.add, ALU.mult).then_inc(uu, 1)
            step(dve.tensor_tensor(gate_i, gate_i, xc, ALU.mult))
            dve.wait_ge(rooted, 1)
            step(dve.tensor_tensor(gate_i, gate_i, r, ALU.mult))
            for c in range(CH):
                m = dve.tensor_tensor_scan(th[:, c, :], a[:, c, :], gate_i[:, c, :], 0.0, ALU.mult, ALU.add)
            step(m)
            dve.wait_ge(silued, 1)
            dve.tensor_tensor(k.mix3[:, 0:CH, :], th, z, ALU.mult).then_inc(done, 1)

        @block.tensor
        def _(pe):
            pe.wait_ge(conv_done, 1)
            pe.wait_ge(arrived, 48)
            for c in range(CH):
                for g, w in enumerate((wa, wx)):
                    m = pe.matmul(B[c][:, g * T:(g + 1) * T], w[:, c, :], xc[:, c, :], start=True, stop=True)
                m.then_inc(gates_in, 1)

        @block.scalar
        def _(act):
            act.wait_ge(e_asked, 1)
            act.activation(size, e, ACT.Exp).then_inc(e_done, 1)
            act.activation(z, z, ACT.Silu).then_inc(silued, 1)
            for c in range(CH):
                act.wait_ge(gates_in, c + 1)
                act.activation(r[:, c, :], B[c][:, 0:T], ACT.Sigmoid, bias=ba[:, c:c + 1]).then_inc(gates_out, 1)
                act.activation(gate_i[:, c, :], B[c][:, T:2 * T], ACT.Sigmoid, bias=bx[:, c:c + 1]).then_inc(gates_out, 1)
            act.wait_ge(dec_done, 1)
            act.wait_ge(gates_out, 2 * CH)
            for c in range(CH):
                act.activation(th[:, c, :], r[:, c, :], ACT.Tanh, scale=growth[:, c:c + 1]).then_inc(exps, 1)
            for c in range(CH):
                act.activation(a[:, c, :], r[:, c, :], ACT.Exp, scale=decay[:, c:c + 1]).then_inc(exps, 1)
            act.wait_ge(uu, 1)
            act.activation(r[:, :, :], th[:, :, :], ACT.Sqrt).then_inc(rooted, 1)



def mlstm(k, ml, name="ml"):
    nc, ins, B = k.nc, k.ins, k.banks
    u = shaped(k.h[0:ML_C, S_ML_U:S_ML_U + MLC * T], MLC, T)
    tok = shaped(k.h[:, S_TOK:S_TOK + NT * TOK_W], NT, TOK_W)
    gates = shaped(k.work[:, 6128:6144], NT, 8)
    bd, bias, cols = ml.bd, ml.bias, ml.cols
    spare = Area(k.mix_t[:, 4 * T:])
    d_sb = spare.take(NT, ML_H, P)
    s_sb = spare.take(NT, ML_H, P)
    uc = shaped(k.h[0:ML_C, 0:MLC * T], MLC, T)
    num = shaped(k.h[:, 0:NT * ML_W], NT * ML_H, ML_DH)
    area = Area(k.act_t[:, :])
    q_t, k_t = (area.take(MLC, T, parts=ML_C) for _ in range(2))
    area = Area(k.work[:, 0:5648], ml.rest.aps[0][:, ml.rest.used[0]:])
    VW = ML_DH + 1
    k_w = area.take(ML_W)
    v = area.take(NT, ML_H, VW)
    c_st = area.take(ML_H, 2, VW, parts=ML_C)
    norm_g = area.take(ML_W)
    s_t = area.take(NT, ML_H, P)
    conv_w, conv_b = shaped(cols[:, 0:MLC * TAPS], MLC, TAPS), cols[:, MLC * TAPS:]
    z, size, log = area.take(NT, 4), area.take(NT, 4), area.take(NT, 4)
    lf = area.take(NT, 4)
    ig = area.take(NT, 4)
    gb = area.take(2, NT, 4)
    c_row = area.take(NT, 4)
    a0, m_new, w0, scale_c = area.take(4), area.take(4), area.take(4), area.take(4)
    m_loc = area.take(4)
    top4, diag4 = area.take(1, parts=4), area.take(4, parts=4)
    m_prev = area.take(NT, 4)
    big, neg_big, s_int, em, den, rden = (area.take(NT, 4) for _ in range(6))
    mean, var, sd = area.take(8), area.take(8), area.take(8)
    S = lambda n: k.sem(f"{name}_{n}")

    arrived, own, conv_done, silued = (S(n) for n in ("arrived", "own", "conv_done", "silued"))
    v_in, v_out, q_in, q_out, k_in, k_out, kt_in, kt_out = (S(n) for n in (
        "v_in", "v_out", "q_in", "q_out", "k_in", "k_out", "kt_in", "kt_out"))
    sized, logged, lf_done, sums, sums_out, a_done, a_turned, diag_done, m_spread, w_asked, w_done = (S(n) for n in (
        "sized", "logged", "lf_done", "sums", "sums_out", "a_done", "a_turned", "diag_done", "m_spread", "w_asked", "w_done"))
    with nc.Block() as block:
        @block.sync
        def _(sp):
            sp.dma_start(norm_g, ins["ml_rows"][:, 8:8 + ML_W]).then_inc(arrived, 16)

        @block.gpsimd
        def _(pool):
            pool.memset(v[:, :, :, ML_DH:VW], 1.0)

        @block.vector
        def _(dve):
            step = Chain(dve, own)
            conv(dve, step, uc, u, conv_w, conv_b, MLC)
            dve.tensor_tensor(z, gates[:, :, 4:8], bias[:, 4:8].unsqueeze(1).to_broadcast([P, NT, 4]), ALU.add).then_inc(conv_done, 1)
            step(dve.tensor_tensor(ig, gates[:, :, 0:4], bias[:, 0:4].unsqueeze(1).to_broadcast([P, NT, 4]), ALU.add))
            dve.scalar_tensor_tensor(size, z, -1.0, z, ALU.mult, ALU.max).then_inc(sized, 1)
            dve.wait_ge(logged, 2)
            dve.scalar_tensor_tensor(lf, z, 0.0, log, ALU.min, ALU.subtract).then_inc(lf_done, 1)
            for b in range(4):
                dve.wait_ge(v_in, b + 1)
                dve.tensor_copy(v[:, b // 2, 2 * (b % 2):2 * (b % 2) + 2, 0:ML_DH], shaped(B[b][:, 0:2 * ML_DH], 2, ML_DH)) \
                   .then_inc(v_out, 1)
            dve.wait_ge(sums, 1)
            step(dve.tensor_copy(gb.rearrange("p a b c -> p (a b c)"), B[6][:, 0:16]))
            dve.tensor_tensor(c_row, ig, gb[:, 0, :, :], ALU.subtract).then_inc(sums_out, 1)
            dve.wait_ge(sums_out, 1)
            dve.tensor_tensor(a0, c_row[:, 0, :], gb[:, 1, 0, :], ALU.add).then_inc(a_done, 1)
            dve.wait_ge(a_turned, 1)
            step(dve.tensor_reduce(top4, B[7][0:4, 0:P], AX.X, ALU.max))
            dve.tensor_scalar(diag4, k.c("ident")[0:4, 0:4], top4, None, ALU.mult).then_inc(diag_done, 1)
            dve.wait_ge(m_spread, 1)
            step(dve.tensor_copy(m_loc, B[6][:, 16:20]))
            step(dve.tensor_tensor(m_new, gb[:, 1, 0, :], m_loc, ALU.max))
            dve.memset(m_prev[:, 0, :], 0.0)
            dve.tensor_copy(m_prev[:, 1, :], m_new)
            step(dve.tensor_tensor(scale_c, m_loc, m_new, ALU.subtract))
            dve.tensor_tensor(w0, a0, m_loc, ALU.subtract).then_inc(w_asked, 1)
            for b in range(4):
                dve.wait_ge(k_in, b + 1)
                dve.tensor_scalar(k_t[:, 2 * b:2 * b + 2, :].rearrange("p a b -> p (a b)"), B[b][0:ML_C, :], ML_DH ** -0.5, None,
                                  ALU.mult).then_inc(k_out, 1)
            dve.wait_ge(w_done, 1)
            for b in range(2):
                dve.wait_ge(kt_in, b + 1)
                for e in range(2):
                    hh = 2 * b + e
                    m = dve.tensor_scalar(k_w[:, hh * ML_DH:(hh + 1) * ML_DH], B[4 + b][:, e * ML_DH:(e + 1) * ML_DH],
                                          ML_DH ** -0.5, w0[:, hh:hh + 1], ALU.mult, ALU.mult)
                m.then_inc(kt_out, 1)

        @block.tensor
        def _(pe):
            for b in range(4):
                for i in range(4):
                    c = 4 * (b % 2) + i
                    m = pe.matmul(B[b][:, i * ML_C:(i + 1) * ML_C], u[:, c, (b // 2) * P:(b // 2 + 1) * P], bd[:, 2, c, :],
                                  start=True, stop=True)
                m.then_inc(v_in, 1)
            pe.wait_ge(lf_done, 1)
            flat = lf.rearrange("p a b -> p (a b)")
            pe.matmul(B[6][:, 0:8], k.c("tri"), flat, start=True, stop=True)
            pe.matmul(B[6][:, 8:16], k.c("ones"), flat, start=True, stop=True).then_inc(sums, 1)
            pe.wait_ge(a_done, 1)
            pe.transpose(B[7][0:4, 0:P], a0, k.c("ident")).then_inc(a_turned, 1)
            pe.wait_ge(diag_done, 1)
            pe.matmul(B[6][:, 16:20], k.c("ones")[0:4, :], diag4, start=True, stop=True).then_inc(m_spread, 1)
            pe.wait_ge(silued, 1)
            pe.wait_ge(w_asked, 1)
            for b in range(4):
                for e in range(2):
                    m = pe.matmul(B[4 + b][0:ML_C, e * T:(e + 1) * T], bd[:, 0, 2 * b + e, :], uc[:, 2 * b + e, :], start=True, stop=True)
                m.then_inc(q_in, 1)
            for b in range(4):
                pe.wait_ge(v_out, 4)
                for e in range(2):
                    m = pe.matmul(B[b][0:ML_C, e * T:(e + 1) * T], bd[:, 1, 2 * b + e, :], uc[:, 2 * b + e, :], start=True, stop=True)
                m.then_inc(k_in, 1)
            for b in range(2):
                pe.wait_ge(q_out, b + 1)
                for i in range(4):
                    c = 4 * b + i
                    m = pe.matmul(B[4 + b][:, i * ML_C:(i + 1) * ML_C], uc[:, c, 0:P], bd[:, 1, c, :], start=True, stop=True)
                m.then_inc(kt_in, 1)

        @block.scalar
        def _(act):
            act.wait_ge(conv_done, 1)
            act.activation(uc, uc, ACT.Silu).then_inc(silued, 1)
            act.wait_ge(sized, 1)
            act.activation(size, size, ACT.Exp, scale=-1.0).then_inc(logged, 1)
            act.wait_ge(logged, 1)
            act.activation(log, size, ACT.Ln, bias=1.0).then_inc(logged, 1)
            mo_z = k.h[:, S_MO_Z:S_MO_Z + MO_H * T]
            act.activation(mo_z, mo_z, ACT.Silu)
            act.activation(tok[:, :, ML_W:2 * ML_W], tok[:, :, ML_W:2 * ML_W], ACT.Silu)
            act.activation(tok[:, :, 0:ML_W], tok[:, :, 0:ML_W], ACT.Sigmoid)
            act.wait_ge(w_asked, 1)
            act.activation(scale_c, scale_c, ACT.Exp).then_inc(w_done, 1)
            act.activation(w0, w0, ACT.Exp).then_inc(w_done, 1)
            for b in range(4):
                act.wait_ge(q_in, b + 1)
                act.activation(q_t[:, 2 * b:2 * b + 2, :].rearrange("p a b -> p (a b)"), B[4 + b][0:ML_C, :], ACT.Copy).then_inc(q_out, 1)

    own2, rowed, d_done, topped, exped, scored, weighted, turned, taken, summed, state_in, state_out, n_done = (S(n) for n in (
        "own2", "rowed", "d_done", "topped", "exped", "scored", "weighted", "turned", "taken", "summed", "state_in",
        "state_out", "n_done"))
    diag_c = S("diag_c")
    with nc.Block() as block:
        @block.vector
        def _(dve):
            step = Chain(dve, own2)
            for t in range(NT):
                dve.tensor_tensor(s_sb[:, t, :, :], k.c("ident").unsqueeze(1).to_broadcast([P, ML_H, P]),
                                  c_row[:, t, :].unsqueeze(2).to_broadcast([P, ML_H, P]), ALU.mult).then_inc(diag_c, 1)
            for t in range(NT):
                dve.wait_ge(rowed, t + 1)
                step(dve.tensor_tensor(d_sb[:, t, :, :].rearrange("p a b -> p (a b)"), B[t][:, :], k.c("causal"), ALU.add))
                step(dve.tensor_reduce(big[:, t, :], d_sb[:, t, :, :], AX.X, ALU.max))
                step(dve.tensor_tensor(big[:, t, :], big[:, t, :], m_prev[:, t, :], ALU.max))
                dve.tensor_tensor(s_int[:, t, :], m_prev[:, t, :], big[:, t, :], ALU.subtract)
                dve.tensor_scalar(neg_big[:, t, :], big[:, t, :], -1.0, None, ALU.mult)
                dve.scalar_tensor_tensor(em[:, t, :], gb[:, 0, t, :], -1.0, big[:, t, :], ALU.mult, ALU.subtract).then_inc(topped, 1)
            for h in range(ML_H):
                dve.wait_ge(state_in, h + 1)
                dve.tensor_scalar(c_st[:, h, :, :].rearrange("p a b -> p (a b)"), B[4 + h][0:ML_C, 0:2 * VW], scale_c[0:ML_C, h:h + 1], None,
                                  ALU.mult).then_inc(state_out, 1)
            for t in range(NT):
                dve.wait_ge(scored, t + 1)
                dve.wait_ge(exped, 6 * t + 6)
                dve.tensor_tensor(s_sb[:, t, :, :].rearrange("p a b -> p (a b)"), B[2 + t][:, :],
                                  d_sb[:, t, :, :].rearrange("p a b -> p (a b)"), ALU.mult).then_inc(weighted, 1)
            for t in range(NT):
                dve.wait_ge(turned, t + 1)
                dve.tensor_copy(s_t[:, t, :, :].rearrange("p a b -> p (a b)"), B[t][:, :]).then_inc(taken, 1)
            for t in range(NT):
                for b in range(2):
                    dve.wait_ge(summed, 2 * t + b + 1)
                    src = shaped(B[2 + 2 * t + b][:, 0:2 * VW], 2, VW)
                    i = 4 * t + 2 * b
                    dve.tensor_copy(num[:, i:i + 2, :], src[:, :, 0:ML_DH])
                    m = dve.tensor_copy(den[:, t, 2 * b:2 * b + 2].unsqueeze(2), src[:, :, ML_DH:VW])
            step(m)
            for h in range(ML_H):
                dve.wait_ge(n_done, h // 2 + 1)
                src = B[(0, 1)[h // 2]][:, (h % 2) * VW:(h % 2 + 1) * VW]
                dve.scalar_tensor_tensor(num[:, 4 + h, :], src[:, 0:ML_DH], s_int[:, 1, h:h + 1], num[:, 4 + h, :], ALU.mult, ALU.add)
                m = dve.scalar_tensor_tensor(den[:, 1, h:h + 1], src[:, ML_DH:VW], s_int[:, 1, h:h + 1], den[:, 1, h:h + 1],
                                             ALU.mult, ALU.add)
            step(m)
            step(dve.scalar_tensor_tensor(rden, den, -1.0, den, ALU.mult, ALU.max))
            step(dve.tensor_tensor(den, rden, em, ALU.max))
            step(dve.reciprocal(rden, den))

        @block.tensor
        def _(pe):
            for t in range(NT):
                pe.wait_ge(diag_c, t + 1)
                pe.matmul(B[t][:, :], k.c("ones"), s_sb[:, t, :, :].rearrange("p a b -> p (a b)"), start=True, stop=True).then_inc(rowed, 1)
            for t in range(NT):
                for h in range(ML_H):
                    for e in range(2):
                        m = pe.matmul(B[2 + t][:, h * P:(h + 1) * P], q_t[:, 2 * h + e, t * P:(t + 1) * P],
                                      k_t[:, 2 * h + e, t * P:(t + 1) * P], start=e == 0, stop=e == 1)
                m.then_inc(scored, 1)
            for h in range(ML_H):
                for e in range(2):
                    m = pe.matmul(B[4 + h][0:ML_C, e * VW:(e + 1) * VW], k_w[:, h * ML_DH + e * ML_C:h * ML_DH + (e + 1) * ML_C],
                                  v[:, 0, h, :], start=True, stop=True)
                m.then_inc(state_in, 1)
            for t in range(NT):
                pe.wait_ge(weighted, t + 1)
                for h in range(ML_H):
                    m = pe.transpose(B[t][:, h * P:(h + 1) * P], s_sb[:, t, h, :], k.c("ident"))
                m.then_inc(turned, 1)
            pe.wait_ge(state_out, 4)
            for t in range(NT):
                pe.wait_ge(taken, t + 1)
                for h in range(ML_H):
                    m = pe.matmul(B[2 + 2 * t + h // 2][:, (h % 2) * VW:(h % 2 + 1) * VW], s_t[:, t, h, :], v[:, t, h, :],
                                  start=True, stop=True)
                    if h % 2:
                        m.then_inc(summed, 1)
            for h in range(ML_H):
                for e in range(2):
                    m = pe.matmul(B[h // 2][:, (h % 2) * VW:(h % 2 + 1) * VW], q_t[:, 2 * h + e, P:2 * P], c_st[:, h, e, :],
                                  start=e == 0, stop=e == 1)
                if h % 2:
                    m.then_inc(n_done, 1)

        @block.scalar
        def _(act):
            for t in range(NT):
                act.wait_ge(topped, t + 1)
                for h in range(ML_H):
                    act.activation(d_sb[:, t, h, :], d_sb[:, t, h, :], ACT.Exp, bias=neg_big[:, t, h:h + 1]).then_inc(exped, 1)
                act.activation(s_int[:, t, :], s_int[:, t, :], ACT.Exp).then_inc(exped, 1)
                act.activation(em[:, t, :], em[:, t, :], ACT.Exp).then_inc(exped, 1)

    own3, meaned, rooted, y_done, y_turned, y_out, y_out2, squared = (S(n) for n in ("own3", "meaned", "rooted", "y_done", "y_turned", "y_out", "y_out2", "squared"))
    sq = shaped(k.act_t[:, 0:NT * ML_W], NT * ML_H, ML_DH)
    with nc.Block() as block:
        @block.vector
        def _(dve):
            step = Chain(dve, own3)
            dve.wait_ge(arrived, 16)
            wide = lambda a: a.unsqueeze(2).to_broadcast([P, NT * ML_H, ML_DH])
            for t in range(NT):
                for h in range(ML_H):
                    i = t * ML_H + h
                    m = dve.scalar_tensor_tensor(num[:, i, :], num[:, i, :], rden[:, t, h:h + 1], tok[:, t, h * ML_DH:(h + 1) * ML_DH],
                                                 ALU.mult, ALU.mult)
            step(m)
            step(dve.tensor_reduce(mean, num, AX.X, ALU.add))
            step(dve.tensor_scalar(mean, mean, 1.0 / ML_DH, None, ALU.mult))
            dve.tensor_tensor(num, num, wide(mean), ALU.subtract).then_inc(meaned, 1)
            dve.wait_ge(squared, 1)
            step(dve.tensor_reduce(var, sq, AX.X, ALU.add))
            dve.tensor_scalar(var, var, 1.0 / ML_DH, LN_EPS, ALU.mult, ALU.add).then_inc(meaned, 1)
            dve.wait_ge(rooted, 1)
            step(dve.reciprocal(var, sd))
            step(dve.tensor_tensor(num, num, wide(var), ALU.mult))
            for t in range(NT):
                y = num[:, 4 * t:4 * t + 4, :].rearrange("p a b -> p (a b)")
                step(dve.tensor_tensor(y, y, norm_g, ALU.mult))
                dve.tensor_tensor(y, y, tok[:, t, ML_W:2 * ML_W], ALU.mult).then_inc(y_done, 1)
            for b in (1, 3, 5):
                dve.wait_ge(y_turned, b + 1)
                dve.tensor_copy(k.mix3[:, 4 + b, :], B[b][:, 0:T]).then_inc(y_out2, 1)

        @block.tensor
        def _(pe):
            pe.wait_ge(y_done, NT)
            flat = shaped(k.h[:, 0:NT * ML_W], NT, ML_W)
            for b in range(ML_W // P):
                for t in range(NT):
                    m = pe.transpose(B[b][:, t * P:(t + 1) * P], flat[:, t, b * P:(b + 1) * P], k.c("ident"))
                m.then_inc(y_turned, 1)

        @block.scalar
        def _(act):
            act.wait_ge(meaned, 1)
            act.activation(sq, num, ACT.Square).then_inc(squared, 1)
            act.wait_ge(meaned, 2)
            act.activation(sd, var, ACT.Sqrt).then_inc(rooted, 1)
            for b in (0, 2, 4):
                act.wait_ge(y_turned, b + 1)
                act.activation(k.mix3[:, 4 + b, :], B[b][:, 0:T], ACT.Copy).then_inc(y_out, 1)


def last_norm(k, name="final"):
    nc = k.nc
    gain = k.act_t[:, 0:D]
    y = shaped(k.h[:, 0:NT * D], NT, D)
    area = Area(k.work[:, :])
    ms, sd, inv = area.take(NT), area.take(NT), area.take(NT)
    arrived, squared, meaned, rooted, own, done, stored = (k.sem(f"{name}_{n}") for n in (
        "arrived", "squared", "meaned", "rooted", "own", "done", "stored"))
    with nc.Block() as block:
        @block.sync
        def _(sp):
            sp.dma_start(gain, k.ins["final_row"]).then_inc(arrived, 16)
            for t in range(NT):
                sp.wait_ge(done, t + 1)
                sp.dma_start(k.out[t * P:(t + 1) * P, :], y[:, t, :]).then_inc(stored, 16)
            sp.wait_ge(stored, 16 * NT)

        @block.scalar
        def _(act):
            for t in range(NT):
                act.activation(y[:, t, :], k.x3[:, t, :], ACT.Square, accum_out=ms[:, t:t + 1]).then_inc(squared, 1)
            act.wait_ge(meaned, 1)
            act.activation(sd, inv, ACT.Sqrt).then_inc(rooted, 1)

        @block.vector
        def _(dve):
            dve.wait_ge(squared, NT)
            dve.tensor_scalar(inv, ms, 1.0 / D, EPS, ALU.mult, ALU.add).then_inc(meaned, 1)
            dve.wait_ge(rooted, 1)
            dve.reciprocal(inv, sd).then_inc(own, 1)
            dve.wait_ge(own, 1)
            dve.wait_ge(arrived, 16)
            for t in range(NT):
                dve.scalar_tensor_tensor(y[:, t, :], k.x3[:, t, :], inv[:, t:t + 1], gain, ALU.mult, ALU.mult).then_inc(done, 1)



def build(nc, ins, out, where):
    with ExitStack() as ctx:
        k = Program(nc, ctx, ins, out, where)
        h3 = shaped(k.h[:, 0:NT * H_W], NT, H_W)

        gd = shaped(k.h[:, NT * H_W:NT * H_W + NT * 32], NT, 32)
        first_in = [
            Job(ins["w_in_gates"], "tok", k.act3, lambda b, g: gd[:, g, :]),
            Job(ins["w_in_qk"], "tok", k.act3, lambda b, g: h3[:, g, bass.ds(b * 512 + H_QD, 512)]),
            Job(ins["w_in_rest"], "tok", k.act3, lambda b, g: h3[:, g, (b if b < 3 else b + 6) * 512:(b if b < 3 else b + 6) * 512 + 512],
                unroll=1),
        ]
        first_out = Job(ins["w_out"], "tok", k.mix3, lambda b, g: k.x3[:, g, bass.ds(b * 512, 512)],
                        add=lambda b, g: k.x3[:, g, bass.ds(b * 512, 512)])

        def load_x(sp, arrived):
            sp.dma_start(k.x3, ins["x"].rearrange("(t p) d -> p t d", p=P)).then_inc(arrived, 16)
            sp.dma_start(k.const[:, :], ins["consts"]).then_inc(arrived, 16)

        normalise(k, "norm1", k.x3, k.c("norm1_g"), k.act3, load=load_x, upcoming=first_in[0])
        groups = sum(job.blocks * job.groups for job in first_in[:-1])
        project(k, first_in, "in1", upcoming=first_out, beside=dilated_rotate(k, groups))
        gla(k)
        dilated_turn(k)
        dil = shaped(k.work[:, 0:2 * DIL_H * T], 2 * DIL_H, T)
        attend(k, "dilated", DIL_H, lambda h: dil[:, h, :], lambda h: dil[:, DIL_H + h, :],
               lambda h, s: h3[:, s, H_VD + h * HD:H_VD + (h + 1) * HD], lambda h: k.c("logc", NT, T), HD ** -0.5,
               lambda h: k.mix3[:, 4 + h, :], Area(k.act_t[:, :]))
        k.recycle()
        project(k, [first_out], "out1")
        query_in = [k.sem(f"query_in{i}") for i in range(2)]

        def load_queries(sp):
            for head in range(2):
                load_query(sp, k, head, query_in)

        normalise(k, "norm2", k.x3, k.c("norm2_g"), k.act3, beside=load_queries)
        peer(k, query_in)
        k.recycle()

        gates2 = shaped(k.work[:, 6128:6144], NT, 8)
        feat = lambda at, groups: lambda b, g: k.h[:, bass.ds(b * (groups * T) + (at + g * T), T)]
        second_in = [
            Job(ins["w_in_ml_gates"], "tok", k.act3, lambda b, g: gates2[:, g, :]),
            Job(ins["w_in_lru"], "feat", k.act3, feat(S_LRU_X, 4)),
            Job(ins["w_in_ml_u"], "feat", k.act3, lambda b, g: k.h[0:ML_C, bass.ds(b * (4 * T) + (S_ML_U + g * T), T)], m=ML_C),
            Job(ins["w_in_mo"], "feat", k.act3, feat(S_MO_Q, 3)),
            Job(ins["w_in_tok"], "tok", k.act3, lambda b, g: k.h[:, bass.ds(b * 384 + (S_TOK + g * TOK_W), 384)]),
        ]
        second_out = Job(ins["w_out_2"], "tok", k.mix3, lambda b, g: k.x3[:, g, bass.ds(b * 512, 512)],
                         add=lambda b, g: k.x3[:, g, bass.ds(b * 512, 512)])
        normalise(k, "norm_mix", k.x3, k.c("mix_g"), k.act3, upcoming=second_in[0])
        project(k, second_in, "in2", upcoming=second_out)
        ml = MlstmWeights(k)
        rg_lru(k, ml)
        mlstm(k, ml)
        k.recycle()
        tok = shaped(k.h[:, S_TOK:S_TOK + NT * TOK_W], NT, TOK_W)
        mo_q, mo_k, mo_z = (shaped(k.h[:, at:at + MO_H * T], MO_H, T) for at in (S_MO_Q, S_MO_K, S_MO_Z))
        alibi = shaped(k.work[:, 0:MO_H * NT * T], MO_H, NT, T)
        attend(k, "moba", MO_H, lambda h: mo_q[:, h, :], lambda h: mo_k[:, h, :],
               lambda h, s: tok[:, s, 2 * ML_W + h * HD:2 * ML_W + (h + 1) * HD], lambda h: alibi[:, h, :, :], HD ** -0.5,
               lambda h: k.mix3[:, 10 + h, :], Area(k.act_t[:, :]), gate=lambda h: mo_z[:, h, :],
               load=lambda sp, arrived: sp.dma_start(k.work[:, 0:MO_H * NT * T], ins["alibi"]).then_inc(arrived, 16), loads=1)
        mem_q = Job(ins["xa_wq"], "feat", k.act3, lambda b, g: k.h[:, g * T:(g + 1) * T])
        project(k, [second_out], "out2", upcoming=mem_q)
        normalise(k, "norm_xa", k.x3, k.c("xa_g"), k.act3)
        mem_out = Job(ins["xa_wo"], "fold", k.mix3, lambda b, g: k.x3[:, g % NT, g // NT * 512:(g // NT + 1) * 512],
                      add=lambda b, g: k.x3[:, g % NT, g // NT * 512:(g // NT + 1) * 512])
        project(k, [mem_q], "mem_q", upcoming=mem_out)
        attend(k, "memory", XA_H, lambda h: k.h[:, h * T:(h + 1) * T], lambda h: k.mem_kv[:, h * T:(h + 1) * T],
               lambda h, s: k.mem_kv[:, XA_H * T + s * 512 + h * HD:XA_H * T + s * 512 + (h + 1) * HD], None, HD ** -0.5,
               lambda h: k.mix3[:, h, :], Area(k.work[:, :]))
        project(k, [mem_out], "mem_out")
        last_norm(k)


def blocks_of(w, cols):
    kk, n = w.shape
    return np.ascontiguousarray(w.reshape(kk // P, P, n // cols, cols).transpose(2, 1, 0, 3))


def rows(*vectors):
    v = np.concatenate([np.asarray(a).reshape(-1) for a in vectors])
    return np.ascontiguousarray(np.broadcast_to(v[None, :], (P, v.size)))


def columns(v, n=P):
    a = np.asarray(v).reshape(-1, n).T
    return np.ascontiguousarray(np.pad(a, ((0, P - n), (0, 0))))


def lay_out(i):
    a = {}
    w = i["w_in"][0]
    a["w_in_gates"] = blocks_of(w[:, 1024:1056], 32)
    a["w_in_qk"] = blocks_of(w[:, 32 + H_QD:32 + H_VD], 512)
    a["w_in_rest"] = blocks_of(np.concatenate([w[:, :1024], w[:, 1056:32 + H_QD], w[:, 32 + H_VD:]], axis=1), 512)
    up = np.zeros((32, 512), np.float32)
    up[:16, :256], up[16:, 256:] = i["gla_up_f"][0], i["gla_up_b"][0]
    a["gla_up"] = up
    a["gla_rows"] = rows(i["gla_bias_f"], i["gla_bias_b"], i["gla_out_g"])
    a["qk_gain"] = rows(i["q_norm_g"], i["k_norm_g"])
    a["w_out"] = blocks_of(i["w_out"][0], 512)
    a["x"] = i["x"][0]
    a["mem"] = i["mem_2"][0]
    a["xa_wkv"] = np.ascontiguousarray(blocks_of(i["xa_wkv_2"][0], 256)[[0, 2, 1, 3]])
    a["xa_wq"] = blocks_of(i["xa_wq_2"][0], 512)
    a["xa_wo"] = np.ascontiguousarray(i["xa_wo_2"][0].reshape(4, P, 4, 512).transpose(1, 2, 0, 3).reshape(1, P, KC, 512))
    w = i["w_in_2"][0]
    at = np.cumsum([0, LRU_W, LRU_W, ML_W, ML_W, ML_W, ML_H, ML_H, MO_W, MO_W, MO_W, MO_W])
    cut = lambda *ns: np.concatenate([w[:, at[n]:at[n + 1]] for n in ns], axis=1)
    a["w_in_ml_gates"] = blocks_of(cut(5, 6), 8)
    a["w_in_lru"] = blocks_of(cut(0, 1), 512)
    a["w_in_ml_u"] = blocks_of(cut(2), 384)
    a["w_in_mo"] = blocks_of(cut(7, 8, 10), 384)
    a["w_in_tok"] = blocks_of(cut(3, 4, 9), 384)
    a["w_out_2"] = blocks_of(i["w_out_2"][0], 512)
    chunks = lambda v: np.asarray(v).reshape(-1, LRU_W // P, P).transpose(2, 1, 0).reshape(P, -1)
    a["lru_cols"] = np.ascontiguousarray(np.concatenate(
        [chunks(i["lru_conv_w_2"][0])] + [columns(i[n]) for n in ("lru_conv_b_2", "lru_ba_2", "lru_bx_2", "lru_lambda_2")], axis=1))
    a["lru_wa"] = np.ascontiguousarray(i["lru_wa_2"][0].transpose(1, 0, 2))
    a["lru_wx"] = np.ascontiguousarray(i["lru_wx_2"][0].transpose(1, 0, 2))
    a["ml_cols"] = np.ascontiguousarray(np.concatenate(
        [i["ml_conv_w_2"][0].reshape(TAPS, MLC, ML_C).transpose(2, 1, 0).reshape(ML_C, -1), i["ml_conv_b_2"][0].reshape(MLC, ML_C).T], axis=1))
    a["ml_qkv"] = np.ascontiguousarray(np.stack(
        [i[n][0].reshape(MLC, ML_C, 4).transpose(1, 0, 2) for n in ("ml_wq_2", "ml_wk_2", "ml_wv_2")], axis=1))
    a["ml_rows"] = rows(i["ml_bi_2"], i["ml_bf_2"], i["ml_norm_g_2"])
    a["alibi"] = alibi_bias()
    a["final_row"] = rows(i["final_norm_g_2"])
    a["w_query"] = blocks_of(i["peer_w_query"][0], 2 * PEER_K)
    a["sub_keys"] = np.ascontiguousarray(i["peer_sub_keys"][0].transpose(3, 0, 1, 2).reshape(P, 2 * PEER_H, PEER_K))
    a["norm2_row"] = rows(i["norm2_g"])
    a["peer_down"] = i["peer_down"][0]
    a["peer_up"] = i["peer_up"][0]
    parts = chunk_masks()
    for n, v in (("norm1_g", "norm1_g"), ("norm2_g", "norm2_g"), ("mix_g", "mix_norm_g_2"), ("xa_g", "xa_norm_g_2"),
                 ("mem_g", "mem_norm_g_2")):
        parts[n] = columns(i[v])
    a["consts"], where = pack(parts)
    return a, where


def kernel(**inputs):
    from concourse import bacc
    from concourse.bass_utils import run_bass_kernel_spmd

    arrays, where = lay_out({name: np.asarray(a) for name, a in inputs.items()})
    nc = bacc.Bacc("TRN2", target_bir_lowering=False, num_devices=1)
    ins = {name: nc.dram_tensor(f"in_{name}_dram", a.shape, mybir.dt.from_np(a.dtype), kind="ExternalInput").ap()
           for name, a in arrays.items()}
    out = nc.dram_tensor("out_0_dram", [T, D], F32, kind="ExternalOutput").ap()
    build(nc, ins, out, where)
    r = run_bass_kernel_spmd(nc, [{f"in_{name}_dram": a for name, a in arrays.items()}], core_ids=[0])
    return r.results[0]["out_0_dram"].reshape(1, T, D)
```
